# Optimizing a Trainium2 kernel written in Bass

```python
import math
import jax, jax.numpy as jnp
from jax import lax
import numpy as np

D_MODEL = 1024
BATCH = 1
SEQ = 512
DEPTH = 1
DEC_BATCH = 8
DEC_SEQ = 8
PAST_LEN = 2048
PAGE_SIZE = 128

ATT_WIDTH = D_MODEL // 2
SSM_WIDTH = D_MODEL - ATT_WIDTH
HEAD_DIM = 64
N_HEADS = ATT_WIDTH // HEAD_DIM
BRANCHES = ((128, 1), (512, 4), (2048, 16))
MAX_WINDOW = 2048
BLK = 128
SSM_GROUP = 16
N_SSM_GROUPS = SSM_WIDTH // SSM_GROUP
SSM_STATE = 64
DT_MIN = 0.001
DT_MAX = 0.1
PEER_HEADS = 8
N_KEYS = 128
N_EXPERTS = N_KEYS * N_KEYS
PEER_TOPK = 16
D_KEY = 256
PEER_BLOCK = 128
PLE_DIM = 256
ALPHA = (2 * DEPTH) ** 0.25
BETA = (8 * DEPTH) ** -0.25
LN_EPS = 1e-5

kernel_name = "hybrid_s5_dilated_peer_decoder_step"

def _alibi_slopes():
    return 2.0 ** (-8.0 * jnp.arange(1, N_HEADS + 1, dtype=jnp.float32) / N_HEADS)

def _layer_norm(x, g, b):
    xf = x.astype(jnp.float32)
    mu = jnp.mean(xf, -1, keepdims=True)
    var = jnp.mean(jnp.square(xf - mu), -1, keepdims=True)
    return ((xf - mu) * lax.rsqrt(var + LN_EPS)).astype(x.dtype) * g + b

def _rms_norm(x, g):
    xf = x.astype(jnp.float32)
    return (xf * lax.rsqrt(jnp.mean(xf * xf, -1, keepdims=True) + LN_EPS)).astype(x.dtype) * g

def _in_proj(x, w_in, b_in):
    B, T, _ = x.shape
    proj = x @ w_in + b_in
    q, k, v, u = jnp.split(proj, [ATT_WIDTH, 2 * ATT_WIDTH, 3 * ATT_WIDTH], axis=-1)
    heads = lambda t: t.reshape(B, T, N_HEADS, HEAD_DIM)
    return heads(q), heads(k), heads(v), u.reshape(B, T, N_SSM_GROUPS, SSM_GROUP)

def _dilated_branch_prompt(q, k, v, window, dilation, slopes):
    B, S, H, E = q.shape
    L = S // dilation
    steps = window // dilation
    nb = -(-L // BLK)
    Lp = nb * BLK

    def to_sub(t):
        t = t.reshape(B, L, dilation, H, E).transpose(0, 2, 1, 3, 4)
        t = jnp.pad(t, ((0, 0), (0, 0), (0, Lp - L), (0, 0), (0, 0)))
        return t.reshape(B, dilation, nb, BLK, H, E)

    def with_prev(t):
        prev = jnp.pad(t[:, :, :-1], ((0, 0), (0, 0), (1, 0), (0, 0), (0, 0), (0, 0)))
        return jnp.concatenate([prev, t], axis=3)

    qs = to_sub(q)
    kk = with_prev(to_sub(k))
    vv = with_prev(to_sub(v))
    s = jnp.einsum('bdnqhe,bdnkhe->bdnhqk', qs, kk).astype(jnp.float32) * (E ** -0.5)
    qi = jnp.arange(BLK)[:, None]
    kj = jnp.arange(2 * BLK)[None, :]
    delta = qi - kj + BLK
    jglob = jnp.arange(nb)[:, None, None] * BLK - BLK + kj[None]
    valid = (delta >= 0) & (delta <= steps) & (jglob >= 0)
    bias = -slopes[:, None, None] * (dilation * delta).astype(jnp.float32)
    s = jnp.where(valid[None, None, :, None], s + bias[None, None, None], -jnp.inf)
    lse = jax.nn.logsumexp(s, axis=-1)
    p = jnp.exp(s - lse[..., None])
    o = jnp.einsum('bdnhqk,bdnkhe->bdnqhe', p.astype(vv.dtype), vv)
    o = o.reshape(B, dilation, Lp, H, E)[:, :, :L].transpose(0, 2, 1, 3, 4).reshape(B, S, H, E)
    lse = lse.transpose(0, 1, 2, 4, 3).reshape(B, dilation, Lp, H)[:, :, :L]
    lse = lse.transpose(0, 2, 1, 3).reshape(B, S, H)
    return o, lse

def _dilated_branch_sample(q, kc, vc, window, dilation, slopes):
    B, T, H, E = q.shape
    W = kc.shape[1] - T
    steps = window // dilation
    m = jnp.arange(steps + 1)
    rows = W + jnp.arange(T)[:, None] - dilation * m[None, :]
    valid = rows >= 0
    rows = jnp.maximum(rows, 0)
    kg = jnp.take(kc, rows, axis=1)
    vg = jnp.take(vc, rows, axis=1)
    s = jnp.einsum('bthe,btmhe->bhtm', q, kg).astype(jnp.float32) * (E ** -0.5)
    bias = -slopes[:, None, None] * (dilation * m).astype(jnp.float32)[None, None, :]
    s = jnp.where(valid[None, None], s + bias, -jnp.inf)
    lse = jax.nn.logsumexp(s, axis=-1)
    p = jnp.exp(s - lse[..., None])
    o = jnp.einsum('bhtm,btmhe->bthe', p.astype(vg.dtype), vg)
    return o, lse.transpose(0, 2, 1)

def _merge_branches(outs, lses):
    w = jax.nn.softmax(jnp.stack(lses, 0), axis=0)
    return jnp.einsum('rbth,rbthe->bthe', w.astype(outs[0].dtype), jnp.stack(outs, 0))

def _attn_prompt(q, k, v):
    slopes = _alibi_slopes()
    outs, lses = [], []
    for window, dilation in BRANCHES:
        o, l = _dilated_branch_prompt(q, k, v, window, dilation, slopes)
        outs.append(o)
        lses.append(l)
    return _merge_branches(outs, lses)

def _attn_sample(q, kc, vc):
    slopes = _alibi_slopes()
    outs, lses = [], []
    for window, dilation in BRANCHES:
        o, l = _dilated_branch_sample(q, kc, vc, window, dilation, slopes)
        outs.append(o)
        lses.append(l)
    return _merge_branches(outs, lses)

def _ssm(u, h0_re, h0_im, lam_re, lam_im, log_dt, b_re, b_im, c_re, c_im, d_skip):
    f32 = jnp.float32
    dt = jnp.exp(log_dt.astype(f32))[:, None]
    lr, li = lam_re.astype(f32), lam_im.astype(f32)
    mag = jnp.exp(lr * dt)
    a_re = mag * jnp.cos(li * dt)
    a_im = mag * jnp.sin(li * dt)
    den = lr * lr + li * li
    nr = a_re - 1.0
    z_re = (nr * lr + a_im * li) / den
    z_im = (a_im * lr - nr * li) / den
    uf = u.astype(f32)
    bu_re = jnp.einsum('btgp,gnp->btgn', uf, b_re.astype(f32))
    bu_im = jnp.einsum('btgp,gnp->btgn', uf, b_im.astype(f32))
    x_re = z_re * bu_re - z_im * bu_im
    x_im = z_re * bu_im + z_im * bu_re
    h0r, h0i = h0_re.astype(f32), h0_im.astype(f32)
    x_re = x_re.at[:, 0].add(a_re * h0r - a_im * h0i)
    x_im = x_im.at[:, 0].add(a_re * h0i + a_im * h0r)

    def combine(e1, e2):
        a1r, a1i, b1r, b1i = e1
        a2r, a2i, b2r, b2i = e2
        return (a2r * a1r - a2i * a1i, a2r * a1i + a2i * a1r,
                a2r * b1r - a2i * b1i + b2r, a2r * b1i + a2i * b1r + b2i)

    elems = (jnp.broadcast_to(a_re, x_re.shape), jnp.broadcast_to(a_im, x_re.shape), x_re, x_im)
    _, _, h_re, h_im = lax.associative_scan(combine, elems, axis=1)
    y = (jnp.einsum('btgn,gpn->btgp', h_re, c_re.astype(f32))
         - jnp.einsum('btgn,gpn->btgp', h_im, c_im.astype(f32))
         + d_skip.astype(f32) * uf)
    return y, h_re[:, -1], h_im[:, -1]

def _peer(h, w_pq, sub_keys1, sub_keys2, peer_u, peer_v):
    B, T, D = h.shape
    x = h.reshape(B * T, D)
    n = x.shape[0]
    nblk = -(-n // PEER_BLOCK)
    x = jnp.pad(x, ((0, nblk * PEER_BLOCK - n), (0, 0))).reshape(nblk, PEER_BLOCK, D)

    def block(xb):
        q = (xb @ w_pq).reshape(PEER_BLOCK, PEER_HEADS, 2, D_KEY // 2)
        s1 = jnp.einsum('thk,nk->thn', q[:, :, 0], sub_keys1).astype(jnp.float32)
        s2 = jnp.einsum('thk,nk->thn', q[:, :, 1], sub_keys2).astype(jnp.float32)
        v1, i1 = lax.top_k(s1, PEER_TOPK)
        v2, i2 = lax.top_k(s2, PEER_TOPK)
        cand = (v1[..., :, None] + v2[..., None, :]).reshape(PEER_BLOCK, PEER_HEADS, PEER_TOPK * PEER_TOPK)
        sc, ci = lax.top_k(cand, PEER_TOPK)
        e = (jnp.take_along_axis(i1, ci // PEER_TOPK, -1) * N_KEYS
             + jnp.take_along_axis(i2, ci % PEER_TOPK, -1))
        g = jax.nn.softmax(sc, axis=-1)
        u = peer_u[e]
        v = peer_v[e]
        a = jax.nn.gelu(jnp.einsum('td,thkd->thk', xb, u).astype(jnp.float32))
        return jnp.einsum('thk,thkd->td', (g * a).astype(v.dtype), v)

    out = lax.map(block, x)
    return out.reshape(-1, D)[:n].reshape(B, T, D)

def _layer_tail(x, att, ssm_y, p, w_glu, b_glu, g_att_out, g_ssm_out, w_out, b_out,
                ln1_g, ln1_b, w_pq, sub_keys1, sub_keys2, peer_u, peer_v,
                w_ple, w_ple_gate, ln2_g, ln2_b):
    B, T, _ = x.shape
    z = jax.nn.gelu(ssm_y.reshape(B, T, SSM_WIDTH)).astype(x.dtype)
    ssm_out = z * jax.nn.sigmoid(z @ w_glu + b_glu)
    mixed = jnp.concatenate([_rms_norm(att.reshape(B, T, ATT_WIDTH), g_att_out),
                             _rms_norm(ssm_out, g_ssm_out)], axis=-1)
    h = _layer_norm(ALPHA * x + mixed @ w_out + b_out, ln1_g, ln1_b)
    ple = jax.nn.sigmoid(h @ w_ple_gate) * (p @ w_ple)
    ffn = _peer(h, w_pq, sub_keys1, sub_keys2, peer_u, peer_v)
    return _layer_norm(ALPHA * h + ffn + ple, ln2_g, ln2_b)

def setup_inputs(seed: int = 0) -> dict:
    key = jax.random.key(seed)
    ks = jax.random.split(key, 36)
    f32 = jnp.float32
    nrm = lambda i, shape, scale=1.0: scale * jax.random.normal(ks[i], shape, f32)
    w_buf = min(MAX_WINDOW, PAST_LEN)
    L = DEPTH
    col_scale = jnp.concatenate([jnp.ones((2 * ATT_WIDTH,), f32), jnp.full((ATT_WIDTH,), BETA, f32),
                                 jnp.ones((SSM_WIDTH,), f32)])
    return {
        "x_prompt": nrm(0, (BATCH, SEQ, D_MODEL)),
        "x_sample": nrm(1, (DEC_BATCH, DEC_SEQ, D_MODEL)),
        "cache_k": nrm(2, (L, DEC_BATCH, w_buf, N_HEADS, HEAD_DIM)),
        "cache_v": nrm(3, (L, DEC_BATCH, w_buf, N_HEADS, HEAD_DIM), BETA),
        "state_ssm_re": nrm(4, (L, DEC_BATCH, N_SSM_GROUPS, SSM_STATE), 0.5),
        "state_ssm_im": nrm(5, (L, DEC_BATCH, N_SSM_GROUPS, SSM_STATE), 0.5),
        "p_prompt": nrm(6, (L, BATCH, SEQ, PLE_DIM)),
        "p_sample": nrm(7, (L, DEC_BATCH, DEC_SEQ, PLE_DIM)),
        "w_in": nrm(8, (L, D_MODEL, 3 * ATT_WIDTH + SSM_WIDTH), D_MODEL ** -0.5) * col_scale,
        "b_in": nrm(9, (L, 3 * ATT_WIDTH + SSM_WIDTH), 0.02),
        "lam_re": -0.5 + nrm(10, (L, N_SSM_GROUPS, SSM_STATE), 0.01),
        "lam_im": jnp.pi * jnp.arange(SSM_STATE, dtype=f32) + nrm(11, (L, N_SSM_GROUPS, SSM_STATE), 0.01),
        "log_dt": jax.random.uniform(ks[12], (L, N_SSM_GROUPS), f32, math.log(DT_MIN), math.log(DT_MAX)),
        "ssm_b_re": nrm(13, (L, N_SSM_GROUPS, SSM_STATE, SSM_GROUP), (2 * SSM_GROUP) ** -0.5),
        "ssm_b_im": nrm(14, (L, N_SSM_GROUPS, SSM_STATE, SSM_GROUP), (2 * SSM_GROUP) ** -0.5),
        "ssm_c_re": nrm(15, (L, N_SSM_GROUPS, SSM_GROUP, SSM_STATE), (2 * SSM_STATE) ** -0.5),
        "ssm_c_im": nrm(16, (L, N_SSM_GROUPS, SSM_GROUP, SSM_STATE), (2 * SSM_STATE) ** -0.5),
        "ssm_d": nrm(17, (L, N_SSM_GROUPS, SSM_GROUP)),
        "w_glu": nrm(18, (L, SSM_WIDTH, SSM_WIDTH), SSM_WIDTH ** -0.5),
        "b_glu": nrm(19, (L, SSM_WIDTH), 0.02),
        "g_att_out": 1.0 + nrm(20, (L, ATT_WIDTH), 0.02),
        "g_ssm_out": 1.0 + nrm(21, (L, SSM_WIDTH), 0.02),
        "w_out": nrm(22, (L, D_MODEL, D_MODEL), BETA * D_MODEL ** -0.5),
        "b_out": nrm(23, (L, D_MODEL), 0.02),
        "ln1_g": 1.0 + nrm(24, (L, D_MODEL), 0.02),
        "ln1_b": nrm(25, (L, D_MODEL), 0.02),
        "w_pq": nrm(26, (L, D_MODEL, PEER_HEADS * D_KEY), D_MODEL ** -0.5),
        "sub_keys1": nrm(27, (L, N_KEYS, D_KEY // 2), (D_KEY // 2) ** -0.5),
        "sub_keys2": nrm(28, (L, N_KEYS, D_KEY // 2), (D_KEY // 2) ** -0.5),
        "peer_u": nrm(29, (L, N_EXPERTS, D_MODEL), D_MODEL ** -0.5),
        "peer_v": nrm(30, (L, N_EXPERTS, D_MODEL), BETA),
        "w_ple": nrm(31, (L, PLE_DIM, D_MODEL), PLE_DIM ** -0.5),
        "w_ple_gate": nrm(32, (L, D_MODEL, D_MODEL), D_MODEL ** -0.5),
        "ln2_g": 1.0 + nrm(33, (L, D_MODEL), 0.02),
        "ln2_b": nrm(34, (L, D_MODEL), 0.02),
    }

def reference(x_prompt, x_sample, cache_k, cache_v, state_ssm_re, state_ssm_im, p_prompt, p_sample,
              w_in, b_in, lam_re, lam_im, log_dt, ssm_b_re, ssm_b_im, ssm_c_re, ssm_c_im, ssm_d,
              w_glu, b_glu, g_att_out, g_ssm_out, w_out, b_out, ln1_g, ln1_b,
              w_pq, sub_keys1, sub_keys2, peer_u, peer_v, w_ple, w_ple_gate, ln2_g, ln2_b):
    yp, ys = x_prompt, x_sample
    w_keep = min(MAX_WINDOW, x_prompt.shape[1])
    kp_l, vp_l, srp_l, sip_l, ks_l, vs_l, srs_l, sis_l = [], [], [], [], [], [], [], []
    for i in range(DEPTH):
        ssm_params = (lam_re[i], lam_im[i], log_dt[i], ssm_b_re[i], ssm_b_im[i],
                      ssm_c_re[i], ssm_c_im[i], ssm_d[i])
        tail_params = (w_glu[i], b_glu[i], g_att_out[i], g_ssm_out[i], w_out[i], b_out[i],
                       ln1_g[i], ln1_b[i], w_pq[i], sub_keys1[i], sub_keys2[i], peer_u[i], peer_v[i],
                       w_ple[i], w_ple_gate[i], ln2_g[i], ln2_b[i])
        q, k, v, u = _in_proj(yp, w_in[i], b_in[i])
        att = _attn_prompt(q, k, v)
        h0 = jnp.zeros((yp.shape[0], N_SSM_GROUPS, SSM_STATE), jnp.float32)
        sy, hr, hi = _ssm(u, h0, h0, *ssm_params)
        kp_l.append(k[:, -w_keep:])
        vp_l.append(v[:, -w_keep:])
        srp_l.append(hr)
        sip_l.append(hi)
        yp = _layer_tail(yp, att, sy, p_prompt[i], *tail_params)
        q, k, v, u = _in_proj(ys, w_in[i], b_in[i])
        kc = jnp.concatenate([cache_k[i].astype(k.dtype), k], axis=1)
        vc = jnp.concatenate([cache_v[i].astype(v.dtype), v], axis=1)
        att = _attn_sample(q, kc, vc)
        sy, hr, hi = _ssm(u, state_ssm_re[i], state_ssm_im[i], *ssm_params)
        ks_l.append(k)
        vs_l.append(v)
        srs_l.append(hr)
        sis_l.append(hi)
        ys = _layer_tail(ys, att, sy, p_sample[i], *tail_params)
    return (yp, ys, jnp.stack(kp_l), jnp.stack(vp_l), jnp.stack(srp_l), jnp.stack(sip_l),
            jnp.stack(ks_l), jnp.stack(vs_l), jnp.stack(srs_l), jnp.stack(sis_l))


_drawn_inputs = setup_inputs


def setup_inputs(seed=0):
    import zlib

    import numpy as np

    out = dict(_drawn_inputs(seed))
    spreads = {}
    factors = {'lam_re': 4.061,
     'b_glu': 4.82,
     'g_att_out': 2.884,
     'g_ssm_out': 2.812,
     'ln2_g': 2.831,
     'ln2_b': 2.852}
    for name, (base, spread) in spreads.items():
        noise = np.random.default_rng([zlib.crc32(name.encode()), seed]).standard_normal(out[name].shape)
        drawn = base * np.exp(spread * noise) if base else spread * noise
        out[name] = __import__('jax').numpy.asarray(drawn.astype(out[name].dtype))
    for name, factor in factors.items():
        out[name] = (out[name] * factor).astype(out[name].dtype)
    return out
```

```python
from contextlib import ExitStack

import numpy as np
import concourse.bass as bass
from concourse import mybir

F32 = mybir.dt.float32
U32 = mybir.dt.uint32
ALU = mybir.AluOpType
ACT = mybir.ActivationFunctionType
AX = mybir.AxisListType

P = 128
D = 1024
DC = D // P
AW = 512
CT = AW // P
NH, HD = 8, 64
SEQ, NB, NT = 512, 8, 8
ST = NB * NT
TOK = SEQ + ST
QB = SEQ // P
BLOCKS = QB + 1
PAST = 2048
BRANCHES = ((128, 1), (512, 4), (2048, 16))
NG, GC, NS = 32, 16, 64
SJ = NG * NS // P
COLD = (PAST - 512) // 2
NK = COLD + 512
KT = NK // P
SK = NK + ST
PLE = 256
PH, PK = 8, 16
EXP = PH * PK
NKEY = 128
ALPHA = 2.0 ** 0.25
EPS = 1e-5
RING = 8
HALF = RING // 2
STEPS = QB * EXP + EXP // 2
TWO_PI = 2.0 * np.pi
TP_HI = 6.28125
TP_LO = TWO_PI - TP_HI
ROUND = 1.5 * 2.0 ** 23
NEG = -3.0e38


def bytes_of_blocks(b):
    return b * P, (P if b < QB else ST)


def build(nc, A):
    ctx = ExitStack()
    with ctx:
        def sb(name, shape, dt=F32):
            return ctx.enter_context(nc.sbuf_tensor(name, shape, dt))

        def sem(name):
            return ctx.enter_context(nc.semaphore(name))

        W = sb("W", [P, 4, 4096])
        R = sb("R", [P, 16384])
        E = sb("E", [P, 19456])
        Wf = W[:, :, :].rearrange("p a b -> p (a b)")

        def view(base, at, *dims):
            n = int(np.prod(dims))
            v = base[:, at:at + n]
            if len(dims) == 2:
                v = v.rearrange("p (a b) -> p a b", a=dims[0])
            if len(dims) == 3:
                v = v.rearrange("p (a b c) -> p a b c", a=dims[0], b=dims[1])
            return v

        ident = sb("ident", [P, P])
        fold = sb("fold", [P, ST])
        iota = sb("iota", [P, PK])
        ones = sb("ones", [P, 2])
        cols = sb("cols", [P, 28])
        ssq = sb("ssq", [P, 2, BLOCKS])
        mv = sb("mv", [P, BLOCKS, 2])
        rstd = sb("rstd", [P, BLOCKS])
        stats = sb("stats", [P, 12])
        lnrow = sb("lnrow", [P, 4])
        lam = sb("lam", [P, 3, SJ])
        sm = sb("sm", [P, 20, SJ])
        small = sb("small", [P, 16])

        xT = view(E, 0, DC, TOK)
        mixT = xT
        qT = view(E, 4608, CT, TOK)
        kT = view(E, 6912, CT, TOK)
        uT = view(E, 9216, CT, TOK)
        vS = view(E, 11520, BLOCKS, AW)
        zT = view(E, 14080, CT, TOK)
        Craw = view(E, 17408, SJ, 2, 32)
        Csc = view(E, 18432, SJ, 2, 32)
        hS = view(E, 4608, BLOCKS, D)
        hT = view(E, 9728, DC, P)
        ybuf = view(E, 10752, D)
        qpT = view(E, 11776, 2, 512)
        sS = view(E, 12800, 2, 4, NKEY)
        sw = view(E, 13824, 256)
        cand = view(E, 14080, 2, 256)
        oh = view(E, 14592, 64, PK)
        gall = view(E, 15616, STEPS + RING)
        eall = view(E, 16208, STEPS + RING).bitcast(U32)
        tv = view(E, 16800, 2 * PH, PK)
        ti = view(E, 17056, 2 * PH, PK).bitcast(U32)
        tif = view(E, 17312, 2 * PH, PK)
        sc = view(E, 17568, PH, PK)
        ci = view(E, 17696, PH, PK).bitcast(U32)
        cab = view(E, 17824, 2, EXP).bitcast(U32)
        cabf = view(E, 18080, 2, EXP)
        e12 = view(E, 18336, 2, EXP)
        gx = view(E, 18592, PH, PK)
        efl = view(E, 18720, EXP)
        eu = view(E, 18848, EXP).bitcast(U32)
        gsm = view(E, 18976, PH)
        dots = view(E, 19008, 2, HALF)
        gel = view(E, 19016, 2, HALF)
        wts = view(E, 19024, 2, HALF)
        stage = view(E, 19032, 2, HALF).bitcast(U32)
        diag = view(E, 0, RING, P)
        rows2 = view(E, 1024, 2, D)
        basebuf = view(E, 3072, D)
        keysT = view(E, 19040, 2, NKEY)

        pbias = view(R, 0, NH, SEQ)
        tc = view(R, 4096, SJ, P)
        ts = view(R, 6144, SJ, P)
        tm = view(R, 8192, SJ, P)
        wt = [view(R, 10240 + 1024 * i, 1024) for i in range(4)]
        rr = [view(R, 10240 + 512 * i, 4, P) for i in range(6)]
        hh = [[view(R, 13312 + 1024 * n + 512 * c, 4, P) for c in range(2)] for n in range(2)]
        vrow = view(R, 15360, AW)
        poolt1 = view(R, 15360, SJ, ST)
        kcS = [view(R, 5120 * n, CT, NK) for n in range(2)]
        vcS = view(R, 10240, KT, AW)
        rows1 = view(R, 0, 3, D)
        xr = view(R, 3072, BLOCKS, D)
        hp = view(R, 8192, BLOCKS, D)
        sg = [view(R, 8192 + 576 * n, TOK) for n in range(2)]
        sq = view(R, 13312, CT, TOK)
        sgm = view(R, 3072, D)
        bout = [view(R, 4096 + 1024 * n, D) for n in range(2)]
        pT = view(R, 13312, 2, TOK)
        ring = view(R, 0, RING, 2 * D)

        pbuf = view(Wf, 0, 2, SK)
        ptS = view(Wf, 2688, 2, KT * ST + ST)
        atok = view(Wf, 4096, 2, AW)
        qblk = view(Wf, 5120, NB, CT, ST)
        sbias = view(Wf, 7168, NK + NB * ST)
        xs = [view(Wf, 8960 + 1024 * i, SJ, ST) for i in range(2)]
        poolt2 = view(Wf, 11008, SJ, ST)
        Bt = Wf[:, 3 * 4096:4 * 4096].rearrange("p (j x n) -> p j x n", j=SJ, x=2)
        glu = view(Wf, 3 * 4096, CT, 512)
        ple = view(Wf, 3 * 4096 + 2048, 2, D)
        asc = view(Wf, 12032, CT, ST)
        h0 = sb("h0", [P, 2, SJ, NB])
        xs_last = [h0[:, c] for c in range(2)]

        bank = ctx.enter_context(nc.psum_tensor("bank", [P, 8, 512], F32))
        bankf = bank[:, :, :].rearrange("p a b -> p (a b)")

        in_x, in_lam, in_cols, in_const, in_ssm, in_pb, in_vrow = (
            sem(n) for n in ("in_x", "in_lam", "in_cols", "in_const", "in_ssm", "in_pb", "in_vrow"))
        in_w = [sem(f"in_w{i}") for i in range(4)]
        in_Bt, in_sb, in_glu = sem("in_Bt"), sem("in_sb"), sem("in_glu")
        in_k, in_v = [sem("in_k0"), sem("in_k1")], sem("in_v")
        in_rows1, in_xr = sem("in_rows1"), sem("in_xr")
        in_out = [sem(f"in_out{i}") for i in range(2)]
        in_gate = [sem(f"in_gate{i}") for i in range(2)]
        in_pT, in_pq, in_rows2 = sem("in_pT"), sem("in_pq"), sem("in_rows2")
        in_base = sem("in_base")
        base_out = [sem("base_out0"), sem("base_out1")]
        ysem, outs = sem("ysem"), sem("outs")
        proj_full = sem("proj_full")
        q_done, k_done, v_done, u_done = (sem(n) for n in ("q_done", "k_done", "v_done", "u_done"))
        dve_chain, act_chain, pool_chain = sem("dve_chain"), sem("act_chain"), sem("pool_chain")
        trig_arg, trig_done, exp_done = sem("trig_arg"), sem("trig_done"), sem("exp_done")
        ssm_exp_in = sem("ssm_exp_in")
        tables_done = sem("tables_done")
        sc_full, sc_biased, p_ready, p_turned, pt_ready, o_full, o_normed = (
            sem(n) for n in ("sc_full", "sc_biased", "p_ready", "p_turned", "pt_ready", "o_full", "o_normed"))
        at_full, at_done = sem("at_full"), sem("at_done")
        bu_full, bu_used, hs_ready, y_full, y_used = (
            sem(n) for n in ("bu_full", "bu_used", "hs_ready", "y_full", "y_used"))
        ones_set, qblk_zero, qblk_set = sem("ones_set"), sem("qblk_zero"), sem("qblk_set")
        sbu_full, sbu_used, sx_ready, sy_full, sy_used = (
            sem(n) for n in ("sbu_full", "sbu_used", "sx_ready", "sy_full", "sy_used"))
        ss_full, ss_biased, sp_exp, sp_ready, sp_turned, spt_ready, so_full, so_used = (
            sem(n) for n in ("ss_full", "ss_biased", "sp_exp", "sp_ready", "sp_turned", "spt_ready", "so_full", "so_used"))
        z_ready, glu_full, sig_ready, mixed, sq_full, ssq_ready, rms_root, rms_ready = (
            sem(n) for n in ("z_ready", "glu_full", "sig_ready", "mixed", "sq_full", "ssq_ready", "rms_root", "rms_ready"))
        out_full, out_used, var_ready, ln_root, h_ready = (
            sem(n) for n in ("out_full", "out_used", "var_ready", "ln_root", "h_ready"))
        ht_full, ht_ready, gate_full, ple_full, gate_sig, base_made = (
            sem(n) for n in ("ht_full", "ht_ready", "gate_full", "ple_full", "gate_sig", "base_made"))
        ple_used = sem("ple_used")
        pq_full, pq_ready, s_full, s_ready, s_used = (
            sem(n) for n in ("pq_full", "pq_ready", "s_full", "s_ready", "s_used"))
        gx_ready, gexp_done, picked, packed = (sem(n) for n in ("gx_ready", "gexp_done", "picked", "packed"))
        hdup = sem("hdup")
        staged, granted, slot_free, dotted, gelued, weighed, diagonal = (
            sem(n) for n in ("staged", "granted", "slot_free", "dotted", "gelued", "weighed", "diagonal"))
        landed = [sem(f"landed{r}") for r in range(RING)]
        y_var, y_root, y_made = sem("y_var"), sem("y_root"), sem("y_made")
        acc_used = sem("acc_used")

        PROJ = ([("q", c) for c in range(CT)] + [("k", c) for c in range(CT)]
                + [("v", b) for b in range(BLOCKS)] + [("u", c) for c in range(CT)])
        UNITS = [(qb, h) for qb in range(QB) for h in range(NH)]

        block = ctx.enter_context(nc.Block())

        @block.sync
        def _(sp):
            def load(dst, src, s):
                sp.dma_start(dst, src).then_inc(s, 16)

            load(xT, A["xT"], in_x)
            load(W[:, 0, :], A["w_in"][0], in_w[0])
            load(lam[:, :, :], A["lam"], in_lam)
            load(cols[:, :], A["cols"], in_cols)
            load(W[:, 1, :], A["w_in"][1], in_w[1])
            load(ident[:, :], A["ident"], in_const)
            load(fold[:, :], A["fold"], in_const)
            load(iota[:, :], A["iota"], in_const)
            load(vrow, A["vrow"], in_vrow)
            load(W[:, 2, :], A["w_in"][2], in_w[2])
            load(Craw, A["Ct"], in_ssm)
            load(h0[:, :, :, :], A["h0"], in_ssm)
            load(W[:, 3, :], A["w_in"][3], in_w[3])
            load(pbias, A["pbias"], in_pb)
            sp.wait_ge(v_done, BLOCKS)
            for b in range(BLOCKS):
                t0, n = bytes_of_blocks(b)
                sp.dma_start(A["v_out"][t0:t0 + n, :], vS[0:n, b, :]).then_inc(outs, 16)
            sp.wait_ge(k_done, CT)
            sp.dma_start(A["k_out"], kT).then_inc(outs, 16)
            sp.wait_ge(proj_full, len(PROJ))
            load(Bt, A["Bt"], in_Bt)
            load(sbias[0:ST], A["sbias"], in_sb)
            sp.wait_ge(sc_biased, len(UNITS))
            sp.wait_ge(y_full, 4 * QB)
            for b in range(NB):
                if b == 2:
                    sp.wait_ge(sbu_full, 2)
                    sp.dma_start(Wf[:, 3 * 4096:4 * 4096], A["glu_ple"]).then_inc(in_glu, 16)
                if b >= 2:
                    sp.wait_ge(ss_full, b - 1)
                load(kcS[b % 2], A["kc"][b][:, :, 0:NK], in_k[b % 2])
                if b >= 1:
                    sp.wait_ge(so_full, b)
                load(vcS, A["vc"][b][:, 0:KT, :], in_v)
            sp.wait_ge(so_full, NB)
            sp.wait_ge(sx_ready, 1)
            load(rows1, A["rows1"], in_rows1)
            for b in range(BLOCKS):
                t0, n = bytes_of_blocks(b)
                load(xr[0:n, b, :], A["x_rows"][t0:t0 + n, :], in_xr)
            sp.wait_ge(sy_full, 1)
            for i in range(2):
                load(W[:, i, :], A["w_out"][i], in_out[i])
            sp.wait_ge(sq_full, 1)
            load(W[:, 2, :], A["w_gate"][0], in_gate[0])
            load(pT, A["pT"], in_pT)
            sp.wait_ge(out_full, BLOCKS)
            load(W[:, 0, :], A["w_gate"][1], in_gate[1])
            sp.wait_ge(hs_ready, 4 * QB + 1)
            sp.dma_start(A["stp_out"], sm[:, 14:16, :]).then_inc(outs, 16)
            for c in range(2):
                sp.dma_start(A["sts_out"][:, c], xs_last[c]).then_inc(outs, 16)
            for b in range(BLOCKS):
                t0, n = bytes_of_blocks(b)
                sp.wait_ge(base_made, b + 1)
                sp.dma_start(A["base"][t0:t0 + n, :], bout[b % 2][0:n, :]).then_inc(base_out[b % 2], 16)
            for i in range(4):
                sp.dma_start(W[:, i, :], A["w_pq"][i]).then_inc(in_pq, 16)
            load(rows2, A["rows2"], in_rows2)
            sp.dma_start(keysT, A["keysT"]).then_inc(in_pq, 16)
            sp.wait_ge(base_out[0], 16 * (BLOCKS - BLOCKS // 2))
            sp.wait_ge(base_out[1], 16 * (BLOCKS // 2))
            c0 = QB * EXP
            sp.dma_start(hS[ST:P, QB, :], hS[0:ST, QB, :]).then_inc(hdup, 16)
            for b in range(BLOCKS):
                t0, n = bytes_of_blocks(b)
                if b > 0:
                    sp.wait_ge(slot_free, RING + EXP * (b - 1) + 1)
                load(basebuf[0:n], A["base"][t0:t0 + n, :], in_base)
                if b == QB - 1:
                    sp.wait_ge(picked, BLOCKS)
                    sp.dma_start(eall[ST:P, c0:c0 + 64], eu[0:ST, 64:128]).then_inc(packed, 16)
                    sp.dma_start(gall[ST:P, c0:c0 + 64], gx[0:ST, 4:8, :].rearrange("p a b -> p (a b)")).then_inc(packed, 16)
                if b > 0:
                    u0, m = bytes_of_blocks(b - 1)
                    sp.wait_ge(y_made, b)
                    sp.dma_start(A["y"][u0:u0 + m, :], ybuf[0:m]).then_inc(ysem, 16)
            u0, m = bytes_of_blocks(BLOCKS - 1)
            sp.wait_ge(y_made, BLOCKS)
            sp.dma_start(A["y"][u0:u0 + m, :], ybuf[0:m]).then_inc(ysem, 16)
            sp.wait_ge(ysem, 16 * BLOCKS)
            sp.wait_ge(outs, 16 * (BLOCKS + 4))

        @block.gpsimd
        def _(pool):
            n_link = [0]

            def link(ins):
                n_link[0] += 1
                ins.then_inc(pool_chain, 1)
                pool.wait_ge(pool_chain, n_link[0])

            nc.gpsimd.memset(ones[:, :], 1.0).then_inc(ones_set, 1)
            pool.wait_ge(proj_full, len(PROJ))
            nc.gpsimd.memset(qblk.rearrange("p a b c -> p (a b c)"), 0.0).then_inc(qblk_zero, 1)

            def wide(k, n):
                return sm[:, k, :].unsqueeze(2).broadcast_to([P, SJ, n])

            pool.wait_ge(tables_done, 1)
            pool.wait_ge(sbu_used, 2)
            tt = nc.gpsimd.tensor_tensor
            link(tt(poolt1, xs[0], wide(10, ST), ALU.mult))
            link(tt(poolt2, xs[1], wide(11, ST), ALU.mult))
            link(tt(poolt1, poolt1, poolt2, ALU.subtract))
            link(tt(poolt2, xs[1], wide(10, ST), ALU.mult))
            link(tt(xs[1], xs[0], wide(11, ST), ALU.mult))
            link(tt(xs[1], xs[1], poolt2, ALU.add))
            link(nc.gpsimd.tensor_copy(xs[0], poolt1))
            vr, vi = (x.rearrange("p j (b t) -> p j b t", t=NT) for x in xs)
            u1, u2 = (x.rearrange("p j (a b) -> p a j b", b=NB) for x in (poolt1, poolt2))
            for t in range(NT):
                pr = h0[:, 0, :, :] if t == 0 else vr[:, :, :, t - 1]
                pi = h0[:, 1, :, :] if t == 0 else vi[:, :, :, t - 1]
                tt(u1[:, 0], pr, wide(0, NB), ALU.mult)
                tt(u1[:, 1], pi, wide(1, NB), ALU.mult)
                tt(u2[:, 0], pi, wide(0, NB), ALU.mult)
                link(tt(u2[:, 1], pr, wide(1, NB), ALU.mult))
                tt(vr[:, :, :, t], vr[:, :, :, t], u1[:, 0], ALU.add)
                link(tt(vi[:, :, :, t], vi[:, :, :, t], u2[:, 0], ALU.add))
                tt(vr[:, :, :, t], vr[:, :, :, t], u1[:, 1], ALU.subtract)
                link(tt(vi[:, :, :, t], vi[:, :, :, t], u2[:, 1], ALU.add))
            nc.gpsimd.tensor_copy(xs_last[0], vr[:, :, :, NT - 1])
            nc.gpsimd.tensor_copy(xs_last[1], vi[:, :, :, NT - 1]).then_inc(sx_ready, 1)

            pool.wait_ge(base_made, BLOCKS)
            pool.wait_ge(base_out[0], 16 * (BLOCKS - BLOCKS // 2))
            pool.wait_ge(base_out[1], 16 * (BLOCKS // 2))
            with pool.Fori(0, STEPS // RING) as i:
                for half in range(2):
                    pool.wait_ge(staged, 2 * i + half + 1)
                    for s in range(HALF):
                        r = half * HALF + s
                        pool.wait_ge(slot_free, i * RING + (r + 1))
                        pool.sem_inc(granted, 1)
                        pool.indirect_dma_start(
                            ring[:, r, :], None, A["uv"],
                            bass.IndirectOffsetOnAxis(ap=stage[:, half, s:s + 1], axis=0),
                        ).then_inc(landed[r], 16)

        @block.tensor
        def _(pe):
            mm = nc.tensor.matmul

            pe.wait_ge(in_x, 16)

            def wait_used(n):
                kind, c = PROJ[n]
                pe.wait_ge({"q": q_done, "k": k_done, "v": v_done, "u": u_done}[kind], c + 1)

            for n, (kind, c) in enumerate(PROJ):
                part = "qkvu".index(kind)
                if c == 0:
                    pe.wait_ge(in_w[part], 16)
                if n >= 2:
                    wait_used(n - 2)
                a, s = bank[:, 2 * (n % 2), :], bank[:, 2 * (n % 2) + 1, 0:ST]
                w = W[:, part, :].rearrange("p (c n) -> p c n", c=DC)
                if kind == "v":
                    t0, m = bytes_of_blocks(c)
                    for k in range(DC):
                        last = mm(a[0:m], xT[:, k, t0:t0 + m], w[:, k, :], start=(k == 0), stop=(k == DC - 1))
                else:
                    for k in range(DC):
                        mm(a, w[:, k, c * P:c * P + P], xT[:, k, 0:SEQ], start=(k == 0), stop=(k == DC - 1))
                    for k in range(DC):
                        last = mm(s, w[:, k, c * P:c * P + P], xT[:, k, SEQ:TOK], start=(k == 0), stop=(k == DC - 1))
                last.then_inc(proj_full, 1)

            def scores(i):
                qb, h = UNITS[i]
                p0, c = 64 * (h % 2), h // 2
                if i >= 2:
                    pe.wait_ge(sc_biased, i - 1)
                mm(bank[:, i % 2, 0:P * (qb + 1)], qT[p0:p0 + 64, c, qb * P:qb * P + P],
                   kT[p0:p0 + 64, c, 0:P * (qb + 1)], start=True, stop=True).then_inc(sc_full, 1)

            def turn_probs(i):
                qb, _ = UNITS[i]
                pe.wait_ge(p_ready, i + 1)
                if i >= 2:
                    pe.wait_ge(pt_ready, i - 1)
                for k in range(qb + 1):
                    last = nc.tensor.transpose(bank[:, 2 + i % 2, k * P:k * P + P],
                                               pbuf[:, i % 2, k * P:k * P + P], ident[:, :])
                last.then_inc(p_turned, 1)

            def values(i):
                qb, h = UNITS[i]
                pe.wait_ge(pt_ready, i + 1)
                if i >= 1:
                    pe.wait_ge(o_normed, i)
                o = bank[:, 4, 0:HD]
                for k in range(qb + 1):
                    last = mm(o, ptS[:, i % 2, k * P:k * P + P], vS[:, k, h * HD:h * HD + HD],
                              start=(k == 0), stop=(k == qb))
                last.then_inc(o_full, 1)

            def turn_att(qb):
                pe.wait_ge(o_normed, NH * (qb + 1))
                pe.wait_ge(y_used, 4 * (qb + 1))
                for c in range(CT):
                    last = nc.tensor.transpose(bank[:, 5, c * P:c * P + P],
                                               atok[:, qb % 2, c * P:c * P + P], ident[:, :])
                last.then_inc(at_full, 1)

            def ssm_in(n):
                b, q = divmod(n, 4)
                if n >= 1:
                    pe.wait_ge(bu_used, n)
                for x in range(2):
                    for j in range(4):
                        last = mm(bank[:, 6 + x, j * P:j * P + P], Bt[:, 4 * q + j, x, :],
                                  uT[:, q, b * P:b * P + P], start=True, stop=True)
                last.then_inc(bu_full, 1)

            def ssm_out(n):
                q = n % 4
                pe.wait_ge(hs_ready, n + 1)
                if n >= 1:
                    pe.wait_ge(y_used, n)
                if n >= 4 and n % 4 == 0:
                    pe.wait_ge(at_done, n // 4)
                for j in range(4):
                    for x in range(2):
                        last = mm(bank[32 * j:32 * j + 32, 5, 0:P], Csc[:, 4 * q + j, x, :],
                                  hh[n % 2][x][:, j, :], start=(x == 0), stop=(x == 1),
                                  skip_group_check=True)
                last.then_inc(y_full, 1)

            pe.wait_ge(q_done, CT)
            pe.wait_ge(k_done, CT)
            pe.wait_ge(v_done, BLOCKS)
            pe.wait_ge(u_done, CT)
            pe.wait_ge(in_const, 16 * 3)
            pe.wait_ge(in_Bt, 16)
            scores(0)
            for i in range(len(UNITS) + 2):
                if i % 2 == 0 and i // 2 < 4 * QB:
                    ssm_in(i // 2)
                if i + 1 < len(UNITS):
                    scores(i + 1)
                if i < len(UNITS):
                    turn_probs(i)
                if 1 <= i <= len(UNITS):
                    values(i - 1)
                if i % 2 == 0 and 1 <= i // 2 <= 4 * QB:
                    ssm_out(i // 2 - 1)
                if i >= 2 and (i - 1) % NH == 0:
                    turn_att((i - 1) // NH - 1)

            pe.wait_ge(y_used, 4 * QB)
            for x in range(2):
                if x == 1:
                    pe.wait_ge(sbu_used, 1)
                for j in range(SJ):
                    last = mm(bankf[:, 6 * 512 + j * ST:6 * 512 + (j + 1) * ST], Bt[:, j, x, :],
                              uT[:, j // 4, SEQ:TOK], start=True, stop=True)
                last.then_inc(sbu_full, 1)

            def s_scores(b):
                pe.wait_ge(in_k[b % 2], 16 * (b // 2 + 1))
                if b >= 1:
                    pe.wait_ge(ss_biased, b)
                for n0 in range(0, NK, 512):
                    n1 = min(n0 + 512, NK)
                    for c in range(CT):
                        mm(bankf[0:ST, n0:n1], qblk[:, b, c, :], kcS[b % 2][:, c, n0:n1],
                           start=(c == 0), stop=(c == CT - 1))
                for c in range(CT):
                    last = mm(bankf[0:ST, NK:SK], qblk[:, b, c, :], kT[:, c, SEQ:TOK],
                              start=(c == 0), stop=(c == CT - 1))
                last.then_inc(ss_full, 1)

            def s_turn(b):
                pe.wait_ge(sp_ready, b + 1)
                if b >= 1:
                    pe.wait_ge(spt_ready, b)
                for k in range(KT + 1):
                    m = P if k < KT else ST
                    last = nc.tensor.transpose(bankf[0:m, 3 * 512 + k * ST:3 * 512 + (k + 1) * ST],
                                               pbuf[0:ST, b % 2, k * P:k * P + m], ident[0:ST, 0:ST])
                last.then_inc(sp_turned, 1)

            def s_values(b):
                pe.wait_ge(spt_ready, b + 1)
                pe.wait_ge(in_v, 16 * (b + 1))
                if b >= 1:
                    pe.wait_ge(so_used, b)
                for c in range(CT):
                    o = bank[:, 5, 64 * (b % 2) + 16 * c:64 * (b % 2) + 16 * c + 16]
                    for k in range(KT + 1):
                        pt = ptS[:, b % 2, k * ST + 16 * c:k * ST + 16 * c + 16]
                        if k < KT:
                            mm(o, vcS[:, k, c * P:c * P + P], pt, start=(k == 0), stop=False)
                        else:
                            last = mm(o, vS[0:ST, QB, c * P:c * P + P], pt[0:ST], start=False, stop=True)
                last.then_inc(so_full, 1)

            pe.wait_ge(qblk_set, 1)
            s_scores(0)
            for b in range(NB):
                if b + 1 < NB:
                    s_scores(b + 1)
                s_turn(b)
                s_values(b)

            pe.wait_ge(sx_ready, 1)
            pe.wait_ge(sbu_used, 2)
            for j in range(SJ):
                p0 = 32 * (j % 4)
                for x in range(2):
                    last = mm(bank[p0:p0 + 32, 6, (j // 4) * ST:(j // 4 + 1) * ST], Craw[:, j, x, :],
                              xs[x][:, j, :], start=(x == 0), stop=(x == 1), skip_group_check=True)
            last.then_inc(sy_full, 1)

            pe.wait_ge(in_glu, 16)
            pe.wait_ge(z_ready, 1)
            for c in range(CT):
                if c >= 2:
                    pe.wait_ge(sig_ready, c - 1)
                for k in range(CT):
                    mm(bank[:, c % 2, :], glu[:, k, c * P:c * P + P], zT[:, k, 0:SEQ],
                       start=(k == 0), stop=(k == CT - 1))
                for k in range(CT):
                    last = mm(bank[:, 2 + c % 2, 0:ST], glu[:, k, c * P:c * P + P], zT[:, k, SEQ:TOK],
                              start=(k == 0), stop=(k == CT - 1))
                last.then_inc(glu_full, 1)

            pe.wait_ge(mixed, CT)
            pe.wait_ge(ones_set, 1)
            for b in range(BLOCKS):
                t0, m = bytes_of_blocks(b)
                for c in range(CT):
                    mm(bank[0:m, 4, b:b + 1], sq[:, c, t0:t0 + m], ones[:, 0:1], start=(c == 0), stop=(c == CT - 1))
            for c in range(CT):
                last = mm(bank[0:ST, 4, 8:9], asc[:, c, :], ones[:, 0:1], start=(c == 0), stop=(c == CT - 1))
            last.then_inc(sq_full, 1)

            pe.wait_ge(at_done, QB)
            pe.wait_ge(ssq_ready, 1)
            for b in range(BLOCKS):
                t0, m = bytes_of_blocks(b)
                if b >= 2:
                    pe.wait_ge(out_used, b - 1)
                for half in range(2):
                    pe.wait_ge(in_out[half], 16)
                    w = W[:, half, :].rearrange("p (c n) -> p c n", c=DC)
                    for part in range(2):
                        for k in range(CT):
                            last = mm(bank[0:m, 4 * (b % 2) + 2 * part + half, :],
                                      mixT[:, CT * part + k, t0:t0 + m], w[:, CT * part + k, :],
                                      start=(k == 0), stop=(k == CT - 1))
                last.then_inc(out_full, 1)

            def turn_h(b, n):
                _, m = bytes_of_blocks(b)
                pe.wait_ge(h_ready, b + 1)
                if n >= 1:
                    pe.wait_ge(ht_ready, n)
                if n > BLOCKS:
                    pe.wait_ge(pq_ready, 4 * (n - BLOCKS))
                    pe.wait_ge(s_ready, 4 * (n - BLOCKS))
                for c in range(DC):
                    last = nc.tensor.transpose(bank[:, c // 4, (c % 4) * P:(c % 4) * P + m],
                                               hS[0:m, b, c * P:c * P + P], ident[0:m, 0:m])
                last.then_inc(ht_full, 1)

            pe.wait_ge(in_gate[0], 16)
            pe.wait_ge(in_gate[1], 16)
            pe.wait_ge(in_pT, 16)
            pe.wait_ge(out_used, BLOCKS)
            for b in range(BLOCKS):
                t0, m = bytes_of_blocks(b)
                turn_h(b, b)
                if b >= 1:
                    pe.wait_ge(ple_used, b)
                for half in range(2):
                    for k in range(2):
                        last = mm(bank[0:m, 4 + half, :], pT[:, k, t0:t0 + m], ple[:, k, half * 512:half * 512 + 512],
                                  start=(k == 0), stop=(k == 1))
                last.then_inc(ple_full, 1)
                pe.wait_ge(ht_ready, b + 1)
                if b >= 1:
                    pe.wait_ge(gate_sig, b)
                for half in range(2):
                    w = W[:, 2 if half == 0 else 0, :].rearrange("p (c n) -> p c n", c=DC)
                    for k in range(DC):
                        last = mm(bank[0:m, 2 + half, :], hT[:, k, 0:m], w[:, k, :], start=(k == 0), stop=(k == DC - 1))
                last.then_inc(gate_full, 1)

            def queries(b):
                t0, m = bytes_of_blocks(b)
                turn_h(b, BLOCKS + b)
                pe.wait_ge(ht_ready, BLOCKS + b + 1)

                def query(c):
                    n = 4 * b + c
                    if n >= 2:
                        pe.wait_ge(pq_ready, n - 1)
                    w = W[:, c, :].rearrange("p (c n) -> p c n", c=DC)
                    for j in range(4):
                        for k in range(DC):
                            last = mm(bank[:, (2, 0)[c % 2], j * P:j * P + m], w[:, k, j * P:j * P + P],
                                      hT[:, k, 0:m], start=(k == 0), stop=(k == DC - 1))
                    last.then_inc(pq_full, 1)

                def score(c):
                    n = 4 * b + c
                    pe.wait_ge(pq_ready, n + 1)
                    if n >= 2:
                        pe.wait_ge(s_ready, n - 1)
                    for j in range(4):
                        last = mm(bank[0:m, (3, 1)[c % 2], j * P:j * P + P], qpT[:, c % 2, j * P:j * P + m],
                                  keysT[:, j % 2, :], start=True, stop=True)
                    last.then_inc(s_full, 1)

                query(0)
                for c in range(4):
                    if c < 3:
                        query(c + 1)
                    score(c)

            def combine(b):
                _, m = bytes_of_blocks(b)
                acc = bankf[0:m, (4 + 2 * (b % 2)) * 512:(6 + 2 * (b % 2)) * 512]
                pe.wait_ge(in_base, 16 * (b + 1))
                if b >= 2:
                    pe.wait_ge(acc_used, b - 1)
                for half in range(2):
                    mm(acc[:, half * 512:half * 512 + 512], ident[0:m, 0:m], basebuf[0:m, half * 512:half * 512 + 512],
                       start=True, stop=False, skip_group_check=True)
                n_it = (EXP if b < QB else EXP // 2) // RING
                i0 = b * EXP // RING
                with pe.Fori(i0, i0 + n_it) as i:
                    for r in range(RING):
                        pe.wait_ge(diagonal, i * RING + (r + 1))
                        for half in range(2):
                            last = mm(acc[:, half * 512:half * 512 + 512], diag[:, r, 0:m],
                                      ring[:, r, D + half * 512:D + half * 512 + 512],
                                      start=False, stop=True, skip_group_check=True)
                        last.then_inc(slot_free, 1)

            pe.wait_ge(in_pq, 16 * 5)
            pe.wait_ge(base_made, BLOCKS)
            pe.sem_inc(slot_free, RING)
            queries(0)
            for b in range(BLOCKS):
                if b + 1 < BLOCKS:
                    queries(b + 1)
                combine(b)

        @block.scalar
        def _(act):
            f = nc.scalar.activation
            n_link = [0]

            def link(ins):
                n_link[0] += 1
                ins.then_inc(act_chain, 1)
                act.wait_ge(act_chain, n_link[0])

            act.wait_ge(in_lam, 16)
            f(sm[:, 2, :], lam[:, 2, :], ACT.Exp).then_inc(exp_done, 1)
            act.wait_ge(ssm_exp_in, 1)
            f(sm[:, 3, :], sm[:, 4, :], ACT.Exp).then_inc(exp_done, 1)
            act.wait_ge(trig_arg, 1)
            f(sm[:, 7:9, :], sm[:, 5:7, :], ACT.Sin).then_inc(trig_done, 1)

            act.wait_ge(in_cols, 16)
            for n, (kind, c) in enumerate(PROJ):
                if kind in "ku":
                    act.wait_ge(proj_full, n + 1)
                    dst, col = (kT, 4 + c) if kind == "k" else (uT, 8 + c)
                    f(dst[:, c, 0:SEQ], bank[:, 2 * (n % 2), :], ACT.Identity, bias=cols[:, col:col + 1])
                    f(dst[:, c, SEQ:TOK], bank[:, 2 * (n % 2) + 1, 0:ST], ACT.Identity,
                      bias=cols[:, col:col + 1]).then_inc(k_done if kind == "k" else u_done, 1)

            act.wait_ge(q_done, CT)
            act.wait_ge(qblk_zero, 1)
            for c in range(CT):
                for e in range(2):
                    last = nc.scalar.copy(
                        qblk[64 * e:64 * e + 64, :, c, (2 * c + e) * NT:(2 * c + e + 1) * NT],
                        qT[64 * e:64 * e + 64, c, SEQ:TOK].rearrange("p (b t) -> p b t", t=NT))
            last.then_inc(qblk_set, 1)

            def exps(i):
                qb, _ = UNITS[i]
                n = P * (qb + 1)
                act.wait_ge(sc_biased, i + 1)
                f(pbuf[:, i % 2, 0:n], pbuf[:, i % 2, 0:n], ACT.Exp, bias=small[:, i % 2:i % 2 + 1],
                  accum_out=small[:, 4 + i % 4:5 + i % 4]).then_inc(p_ready, 1)

            def copy_pt(i):
                qb, _ = UNITS[i]
                n = P * (qb + 1)
                act.wait_ge(p_turned, i + 1)
                if i >= 2:
                    act.wait_ge(o_full, i - 1)
                nc.scalar.copy(ptS[:, i % 2, 0:n], bank[:, 2 + i % 2, 0:n]).then_inc(pt_ready, 1)

            def att_out(qb):
                act.wait_ge(o_normed, NH * (qb + 1))
                link(f(asc.rearrange("p a b -> p (a b)"), atok[:, qb % 2, 0:CT * ST], ACT.Square,
                       accum_out=small[:, 8 + 2 * (qb % 2):9 + 2 * (qb % 2)]))
                f(asc.rearrange("p a b -> p (a b)"), atok[:, qb % 2, CT * ST:AW], ACT.Square,
                  accum_out=small[:, 9 + 2 * (qb % 2):10 + 2 * (qb % 2)])
                act.wait_ge(at_full, qb + 1)
                for c in range(CT):
                    last = f(mixT[:, c, qb * P:qb * P + P], bank[:, 5, c * P:c * P + P], ACT.Copy,
                             scale=cols[:, 16 + c:17 + c])
                last.then_inc(at_done, 1)

            for i in range(len(UNITS) + 2):
                if i < len(UNITS):
                    exps(i)
                if 1 <= i <= len(UNITS):
                    copy_pt(i - 1)
                if i >= 2 and (i - 1) % NH == 0:
                    att_out((i - 1) // NH - 1)

            act.wait_ge(o_full, len(UNITS))
            for x in range(2):
                act.wait_ge(sbu_full, x + 1)
                nc.scalar.copy(xs[x].rearrange("p a b -> p (a b)"), bankf[:, 6 * 512:8 * 512]).then_inc(sbu_used, 1)

            def s_exp(b):
                act.wait_ge(ss_biased, b + 1)
                f(pbuf[0:ST, b % 2, :], pbuf[0:ST, b % 2, :], ACT.Exp, bias=small[0:ST, b % 2:b % 2 + 1],
                  accum_out=small[0:ST, 4 + b % 2:5 + b % 2]).then_inc(sp_exp, 1)

            def s_copy(b):
                act.wait_ge(sp_turned, b + 1)
                if b >= 2:
                    act.wait_ge(so_full, b - 1)
                nc.scalar.copy(ptS[:, b % 2, 0:KT * ST], bankf[:, 3 * 512:3 * 512 + KT * ST])
                nc.scalar.copy(ptS[0:ST, b % 2, KT * ST:(KT + 1) * ST],
                               bankf[0:ST, 3 * 512 + KT * ST:3 * 512 + (KT + 1) * ST]).then_inc(spt_ready, 1)

            s_exp(0)
            for b in range(NB):
                if b + 1 < NB:
                    s_exp(b + 1)
                s_copy(b)

            act.wait_ge(sy_used, 1)
            f(zT.rearrange("p a b -> p (a b)"), zT.rearrange("p a b -> p (a b)"), ACT.Gelu_apprx_tanh).then_inc(z_ready, 1)
            for c in range(CT):
                act.wait_ge(glu_full, c + 1)
                if c >= 2:
                    act.wait_ge(mixed, c - 1)
                f(sg[c % 2][:, 0:SEQ], bank[:, c % 2, :], ACT.Sigmoid, bias=cols[:, 12 + c:13 + c])
                f(sg[c % 2][:, SEQ:TOK], bank[:, 2 + c % 2, 0:ST], ACT.Sigmoid,
                  bias=cols[:, 12 + c:13 + c]).then_inc(sig_ready, 1)

            act.wait_ge(ssq_ready, 1)
            f(ssq[:, :, :], ssq[:, :, :], ACT.Sqrt).then_inc(rms_root, 1)
            act.wait_ge(var_ready, 1)
            f(rstd[:, :], rstd[:, :], ACT.Sqrt).then_inc(ln_root, 1)

            def copy_ht(b, n):
                _, m = bytes_of_blocks(b)
                act.wait_ge(ht_full, n + 1)
                if 1 <= n < BLOCKS:
                    act.wait_ge(gate_full, n)
                if n == BLOCKS:
                    act.wait_ge(gate_full, BLOCKS)
                if n > BLOCKS:
                    act.wait_ge(pq_full, 4 * (n - BLOCKS))
                src = bank[:, 0:2, :].rearrange("p a (b t) -> p (a b) t", b=4)
                nc.scalar.copy(hT[:, :, 0:m], src[:, :, 0:m]).then_inc(ht_ready, 1)

            for b in range(BLOCKS):
                _, m = bytes_of_blocks(b)
                copy_ht(b, b)
                act.wait_ge(gate_full, b + 1)
                if b >= 1:
                    act.wait_ge(ple_used, b)
                f(sgm[0:m], bankf[0:m, 2 * 512:4 * 512], ACT.Sigmoid).then_inc(gate_sig, 1)

            def queries(b):
                _, m = bytes_of_blocks(b)
                copy_ht(b, BLOCKS + b)

                def copy_q(c):
                    n = 4 * b + c
                    act.wait_ge(pq_full, n + 1)
                    if n >= 2:
                        act.wait_ge(s_full, n - 1)
                    src = bank[:, (2, 0)[c % 2], :].rearrange("p (a t) -> p a t", t=P)
                    dst = qpT[:, c % 2, :].rearrange("p (a t) -> p a t", t=P)
                    nc.scalar.copy(dst[:, :, 0:m], src[:, :, 0:m]).then_inc(pq_ready, 1)

                def copy_s(c):
                    n = 4 * b + c
                    act.wait_ge(s_full, n + 1)
                    if n >= 2:
                        act.wait_ge(s_used, n - 1)
                    nc.scalar.copy(sS[0:m, c % 2, :, :].rearrange("p a b -> p (a b)"),
                                   bank[0:m, (3, 1)[c % 2], :]).then_inc(s_ready, 1)

                copy_q(0)
                for c in range(4):
                    if c < 3:
                        copy_q(c + 1)
                    copy_s(c)
                act.wait_ge(gx_ready, b + 1)
                f(gx[0:m], gx[0:m], ACT.Exp).then_inc(gexp_done, 1)

            def copy_stage(half, at):
                return nc.scalar.copy(stage[:, half, :], eall[:, at])

            def weigh(b):
                _, m = bytes_of_blocks(b)
                sel = ident if b < QB else fold
                act.wait_ge(picked, min(b + 2, BLOCKS))
                if b >= QB - 1:
                    act.wait_ge(packed, 32)
                if b == 0:
                    for half in range(2):
                        copy_stage(half, slice(half * HALF, half * HALF + HALF)).then_inc(staged, 1)
                n_it = (EXP if b < QB else EXP // 2) // RING
                i0 = b * EXP // RING
                with act.Fori(i0, i0 + n_it) as i:
                    for half in range(2):
                        act.wait_ge(dotted, 2 * i + half + 1)
                        copy_stage(half, bass.ds(i * RING + (RING + half * HALF), HALF)).then_inc(staged, 1)
                        f(gel[:, half, :], dots[:, half, :], ACT.Gelu_apprx_tanh).then_inc(gelued, 1)
                        act.wait_ge(weighed, 2 * i + half + 1)
                        for s in range(HALF):
                            f(diag[:, half * HALF + s, 0:m], sel[:, 0:m], ACT.Copy,
                              scale=wts[:, half, s:s + 1]).then_inc(diagonal, 1)

            def y_sqrt(b):
                act.wait_ge(y_var, b + 1)
                f(lnrow[:, 2:3], lnrow[:, 1:2], ACT.Sqrt).then_inc(y_root, 1)

            queries(0)
            for b in range(BLOCKS):
                if b + 1 < BLOCKS:
                    queries(b + 1)
                weigh(b)
                y_sqrt(b)

        @block.vector
        def _(dve):
            tt = nc.vector.tensor_tensor
            tsc = nc.vector.tensor_scalar
            stt = nc.vector.scalar_tensor_tensor
            n_link = [0]

            def link(ins):
                n_link[0] += 1
                ins.then_inc(dve_chain, 1)
                dve.wait_ge(dve_chain, n_link[0])

            dve.wait_ge(in_lam, 16)
            dve.wait_ge(exp_done, 1)
            tt(sm[:, 4, :], lam[:, 0, :], sm[:, 2, :], ALU.mult).then_inc(ssm_exp_in, 1)
            link(tt(sm[:, 5, :], lam[:, 1, :], sm[:, 2, :], ALU.mult))
            link(tsc(sm[:, 6, :], sm[:, 5, :], float(np.pi / 2), None, ALU.add))
            th, kk = sm[:, 5:7, :], sm[:, 18:20, :]
            link(tsc(kk, th, float(1 / TWO_PI), ROUND, ALU.mult, ALU.add))
            link(tsc(kk, kk, ROUND, None, ALU.subtract))
            link(stt(th, kk, -TP_HI, th, ALU.mult, ALU.add))
            link(stt(th, kk, -float(TP_LO), th, ALU.mult, ALU.add))
            tsc(th, th, -3.1415925, 3.1415925, ALU.max, ALU.min).then_inc(trig_arg, 1)
            dve.wait_ge(trig_done, 1)
            dve.wait_ge(exp_done, 2)
            tt(sm[:, 0, :], sm[:, 3, :], sm[:, 8, :], ALU.mult)
            link(tt(sm[:, 1, :], sm[:, 3, :], sm[:, 7, :], ALU.mult))
            tt(sm[:, 18, :], lam[:, 0, :], lam[:, 0, :], ALU.mult)
            tt(sm[:, 19, :], lam[:, 1, :], lam[:, 1, :], ALU.mult)
            link(tsc(sm[:, 9, :], sm[:, 0, :], -1.0, None, ALU.add))
            link(tt(sm[:, 18, :], sm[:, 18, :], sm[:, 19, :], ALU.add))
            link(nc.vector.reciprocal(sm[:, 12, :], sm[:, 18, :]))
            tt(sm[:, 10, :], sm[:, 9, :], lam[:, 0, :], ALU.mult)
            tt(sm[:, 11, :], sm[:, 1, :], lam[:, 0, :], ALU.mult)
            tt(sm[:, 18, :], sm[:, 1, :], lam[:, 1, :], ALU.mult)
            link(tt(sm[:, 19, :], sm[:, 9, :], lam[:, 1, :], ALU.mult))
            tt(sm[:, 10, :], sm[:, 10, :], sm[:, 18, :], ALU.add)
            link(tt(sm[:, 11, :], sm[:, 11, :], sm[:, 19, :], ALU.subtract))
            tt(sm[:, 10, :], sm[:, 10, :], sm[:, 12, :], ALU.mult)
            link(tt(sm[:, 11, :], sm[:, 11, :], sm[:, 12, :], ALU.mult))

            def wide(k, n):
                return sm[:, k, :].unsqueeze(2).broadcast_to([P, SJ, n])

            dve.wait_ge(in_ssm, 16 * 2)
            c4 = [w[:, 0:512].rearrange("p (a b) -> p a b", b=32) for w in wt]
            tt(c4[0], Craw[:, :, 0, :], wide(10, 32), ALU.mult)
            tt(c4[1], Craw[:, :, 1, :], wide(11, 32), ALU.mult)
            tt(c4[2], Craw[:, :, 0, :], wide(11, 32), ALU.mult)
            link(tt(c4[3], Craw[:, :, 1, :], wide(10, 32), ALU.mult))
            tt(Csc[:, :, 0, :], c4[0], c4[1], ALU.subtract)
            link(tt(c4[2], c4[2], c4[3], ALU.add))
            tsc(Csc[:, :, 1, :], c4[2], -1.0, None, ALU.mult)
            link(tsc(Craw[:, :, 1, :], Craw[:, :, 1, :], -1.0, None, ALU.mult))

            nc.vector.memset(tc[:, :, 0:1], 1.0)
            nc.vector.memset(ts[:, :, 0:1], 0.0)
            nc.vector.tensor_copy(sm[:, 12, :], sm[:, 8, :])
            nc.vector.tensor_copy(tm, wide(3, P))
            link(nc.vector.tensor_copy(sm[:, 13, :], sm[:, 7, :]))
            nc.vector.memset(tm[:, :, 0:1], 0.0)

            def q_done_job(c):
                n = PROJ.index(("q", c))
                dve.wait_ge(proj_full, n + 1)
                tsc(qT[:, c, 0:SEQ], bank[:, 2 * (n % 2), :], cols[:, c:c + 1], HD ** -0.5, ALU.add, ALU.mult)
                tsc(qT[:, c, SEQ:TOK], bank[:, 2 * (n % 2) + 1, 0:ST], cols[:, c:c + 1], HD ** -0.5,
                    ALU.add, ALU.mult).then_inc(q_done, 1)

            def v_done_job(b):
                _, m = bytes_of_blocks(b)
                n = PROJ.index(("v", b))
                dve.wait_ge(proj_full, n + 1)
                tt(vS[0:m, b, :], bank[0:m, 2 * (n % 2), :], vrow[0:m], ALU.add).then_inc(v_done, 1)

            dve.wait_ge(in_cols, 16)
            dve.wait_ge(in_vrow, 16)
            jobs = [(q_done_job, c) for c in range(CT)] + [(v_done_job, b) for b in range(BLOCKS)]
            n = 1
            while n < P:
                w = [x[:, 0:SJ * n].rearrange("p (a b) -> p a b", b=n) for x in wt]
                tt(w[0], tc[:, :, 0:n], wide(12, n), ALU.mult)
                tt(w[1], ts[:, :, 0:n], wide(13, n), ALU.mult)
                tt(w[2], tc[:, :, 0:n], wide(13, n), ALU.mult)
                link(tt(w[3], ts[:, :, 0:n], wide(12, n), ALU.mult))
                tt(tc[:, :, n:2 * n], w[0], w[1], ALU.subtract)
                tt(ts[:, :, n:2 * n], w[2], w[3], ALU.add)
                tt(sm[:, 18, :], sm[:, 12, :], sm[:, 12, :], ALU.mult)
                tt(sm[:, 19, :], sm[:, 13, :], sm[:, 13, :], ALU.mult)
                link(tt(sm[:, 9, :], sm[:, 12, :], sm[:, 13, :], ALU.mult))
                tt(sm[:, 12, :], sm[:, 18, :], sm[:, 19, :], ALU.subtract)
                link(tsc(sm[:, 13, :], sm[:, 9, :], 2.0, None, ALU.mult))
                n *= 2
                if n > 8 and jobs:
                    fn, c = jobs.pop(0)
                    fn(c)
            nc.vector.memset(small[:, :], 0.0)
            link(nc.vector.memset(ssq[:, :, :], 1.0))
            nc.vector.tensor_copy(sm[:, 9, :], sm[:, 0, :]).then_inc(tables_done, 1)
            for fn, c in jobs:
                fn(c)

            def add_bias(i):
                qb, h = UNITS[i]
                m = P * (qb + 1)
                dve.wait_ge(sc_full, i + 1)
                if i >= 2:
                    dve.wait_ge(p_turned, i - 1)
                link(nc.vector.tensor_tensor_reduce(
                    pbuf[:, i % 2, 0:m], bank[:, i % 2, 0:m], pbias[:, h, SEQ - m:SEQ], 1.0, NEG,
                    ALU.add, ALU.max, small[:, 2 + i % 2:3 + i % 2]))
                tsc(small[:, i % 2:i % 2 + 1], small[:, 2 + i % 2:3 + i % 2], -1.0, None, ALU.mult).then_inc(sc_biased, 1)

            def norm_out(i):
                qb, h = UNITS[i]
                den = small[:, 4 + i % 4:5 + i % 4]
                dve.wait_ge(p_ready, i + 1)
                if h == 0 and qb >= 2:
                    dve.wait_ge(at_done, qb - 1)
                link(nc.vector.reciprocal(small[:, 12 + i % 4:13 + i % 4], den))
                dve.wait_ge(o_full, i + 1)
                tsc(atok[:, qb % 2, h * HD:h * HD + HD], bank[:, 4, 0:HD],
                    small[:, 12 + i % 4:13 + i % 4], None, ALU.mult).then_inc(o_normed, 1)

            def keep_squares(qb):
                dve.wait_ge(at_done, qb + 1)
                tt(ssq[:, 0, qb:qb + 1], small[:, 8 + 2 * (qb % 2):9 + 2 * (qb % 2)],
                   small[:, 9 + 2 * (qb % 2):10 + 2 * (qb % 2)], ALU.add)

            def flat(x):
                return x.rearrange("p a b -> p (a b)")

            def scan(n):
                b, q = divmod(n, 4)
                j = slice(4 * q, 4 * q + 4)
                c_, s_ = tc[:, j, :], ts[:, j, :]
                re = bank[:, 6, :].rearrange("p (a t) -> p a t", t=P)
                im = bank[:, 7, :].rearrange("p (a t) -> p a t", t=P)
                r_re, r_im, t1, t2, t3, t4 = rr
                h_re, h_im = hh[n % 2]
                dve.wait_ge(bu_full, n + 1)
                tt(t1, re, c_, ALU.mult)
                tt(t2, im, s_, ALU.mult)
                tt(t3, im, c_, ALU.mult)
                tt(t4, re, s_, ALU.mult).then_inc(bu_used, 1)
                dve.wait_ge(bu_used, n + 1)
                tt(r_re, t1, t2, ALU.add)
                link(tt(r_im, t3, t4, ALU.subtract))
                if b > 0:
                    tt(r_re[:, :, 0], r_re[:, :, 0], sm[:, 16, j], ALU.add)
                    link(tt(r_im[:, :, 0], r_im[:, :, 0], sm[:, 17, j], ALU.add))
                m = flat(tm[:, j, :])
                nc.vector.tensor_tensor_scan(flat(t1), m, flat(r_re), 0.0, ALU.mult, ALU.add)
                link(nc.vector.tensor_tensor_scan(flat(t2), m, flat(r_im), 0.0, ALU.mult, ALU.add))
                tt(r_re, t1, c_, ALU.mult)
                tt(t3, t2, s_, ALU.mult)
                tt(r_im, t1, s_, ALU.mult)
                link(tt(t4, t2, c_, ALU.mult))
                if n >= 2:
                    dve.wait_ge(y_full, n - 1)
                tt(h_re, r_re, t3, ALU.subtract)
                tt(h_im, r_im, t4, ALU.add).then_inc(hs_ready, 1)
                dve.wait_ge(hs_ready, n + 1)
                k = 0 if b < QB - 1 else 10
                o = 16 if b < QB - 1 else 14
                hl, hi = h_re[:, :, P - 1], h_im[:, :, P - 1]
                tt(sm[:, 18, j], hl, sm[:, k, j], ALU.mult)
                tt(sm[:, 19, j], hi, sm[:, k + 1, j], ALU.mult)
                tt(sm[:, 12, j], hl, sm[:, k + 1, j], ALU.mult)
                link(tt(sm[:, 13, j], hi, sm[:, k, j], ALU.mult))
                tt(sm[:, o, j], sm[:, 18, j], sm[:, 19, j], ALU.subtract)
                link(tt(sm[:, o + 1, j], sm[:, 12, j], sm[:, 13, j], ALU.add))

            def skip_term(n):
                b, q = divmod(n, 4)
                dve.wait_ge(y_full, n + 1)
                stt(zT[:, q, b * P:b * P + P], uT[:, q, b * P:b * P + P], cols[:, 24 + q:25 + q],
                    bank[:, 5, 0:P], ALU.mult, ALU.add).then_inc(y_used, 1)

            dve.wait_ge(in_pb, 16)
            dve.wait_ge(u_done, CT)
            for i in range(len(UNITS) + 2):
                if i < len(UNITS):
                    add_bias(i)
                if 2 <= i:
                    norm_out(i - 2)
                if i % 2 == 0 and i // 2 < 4 * QB:
                    scan(i // 2)
                if i % 2 == 1 and i // 2 >= 1:
                    skip_term(i // 2 - 1)
                if i >= 4 and (i - 3) % NH == 0:
                    keep_squares((i - 3) // NH - 1)
            keep_squares(QB - 1)
            nc.vector.tensor_copy(sm[:, 9, :], sm[:, 0, :]).then_inc(hs_ready, 1)

            def s_bias(b):
                dve.wait_ge(ss_full, b + 1)
                if b >= 2:
                    dve.wait_ge(sp_turned, b - 1)
                nc.vector.tensor_tensor_reduce(
                    pbuf[0:ST, b % 2, 0:NK], bankf[0:ST, 0:NK], sbias[0:ST, 0:NK], 1.0, NEG,
                    ALU.add, ALU.max, small[0:ST, 8:9])
                link(nc.vector.tensor_tensor_reduce(
                    pbuf[0:ST, b % 2, NK:SK], bankf[0:ST, NK:SK], sbias[0:ST, NK + b * ST:NK + (b + 1) * ST], 1.0, NEG,
                    ALU.add, ALU.max, small[0:ST, 9:10]))
                link(tt(small[0:ST, 8:9], small[0:ST, 8:9], small[0:ST, 9:10], ALU.max))
                tsc(small[0:ST, b % 2:b % 2 + 1], small[0:ST, 8:9], -1.0, None, ALU.mult).then_inc(ss_biased, 1)

            def s_norm(b):
                dve.wait_ge(sp_exp, b + 1)
                link(nc.vector.reciprocal(small[0:ST, 12:13], small[0:ST, 4 + b % 2:5 + b % 2]))
                tsc(pbuf[0:ST, b % 2, :], pbuf[0:ST, b % 2, :], small[0:ST, 12:13], None, ALU.mult).then_inc(sp_ready, 1)

            def s_out(b):
                dve.wait_ge(so_full, b + 1)
                for e in range(2):
                    src = bank[64 * e:64 * e + 64, 5, 64 * (b % 2):64 * (b % 2) + 64].rearrange(
                        "p (c x t) -> p c x t", c=CT, x=2)[:, :, e, :]
                    last = nc.vector.tensor_copy(
                        mixT[64 * e:64 * e + 64, 0:CT, SEQ + b * NT:SEQ + (b + 1) * NT], src)
                last.then_inc(so_used, 1)

            dve.wait_ge(in_sb, 16)
            s_bias(0)
            for b in range(NB):
                s_norm(b)
                if b + 1 < NB:
                    s_bias(b + 1)
                s_out(b)
            dve.wait_ge(so_used, NB)
            link(tt(asc, mixT[:, 0:CT, SEQ:TOK], mixT[:, 0:CT, SEQ:TOK], ALU.mult))
            for c in range(CT):
                tsc(mixT[:, c, SEQ:TOK], mixT[:, c, SEQ:TOK], cols[:, 16 + c:17 + c], None, ALU.mult)
            dve.wait_ge(sy_full, 1)
            for q in range(CT):
                last = stt(zT[:, q, SEQ:TOK], uT[:, q, SEQ:TOK], cols[:, 24 + q:25 + q],
                           bank[:, 6, q * ST:(q + 1) * ST], ALU.mult, ALU.add)
            last.then_inc(sy_used, 1)

            for c in range(CT):
                dve.wait_ge(sig_ready, c + 1)
                link(tt(sg[c % 2], sg[c % 2], zT[:, c, :], ALU.mult))
                tt(sq[:, c, :], sg[c % 2], sg[c % 2], ALU.mult)
                tsc(mixT[:, CT + c, :], sg[c % 2], cols[:, 20 + c:21 + c], None, ALU.mult).then_inc(mixed, 1)
            dve.wait_ge(sq_full, 1)
            nc.vector.tensor_copy(ssq[:, 1, 0:QB], bank[:, 4, 0:QB])
            nc.vector.tensor_copy(ssq[0:ST, 1, QB:BLOCKS], bank[0:ST, 4, QB:BLOCKS])
            link(nc.vector.tensor_copy(ssq[0:ST, 0, QB:BLOCKS], bank[0:ST, 4, 8:9]))
            tsc(ssq[:, :, :], ssq[:, :, :], 1.0 / AW, EPS, ALU.mult, ALU.add).then_inc(ssq_ready, 1)
            dve.wait_ge(rms_root, 1)
            link(nc.vector.reciprocal(ssq[:, :, :], ssq[:, :, :]))

            link(nc.vector.memset(mv[:, :, :], 1.0))
            dve.wait_ge(in_rows1, 16)
            dve.wait_ge(in_xr, 16 * BLOCKS)
            for b in range(BLOCKS):
                _, m = bytes_of_blocks(b)
                link(stt(xr[0:m, b, :], xr[0:m, b, :], ALPHA, rows1[0:m, 0, :], ALU.mult, ALU.add))
                dve.wait_ge(out_full, b + 1)
                o = 4 * (b % 2) * 512
                link(stt(xr[0:m, b, :], bankf[0:m, o:o + D], ssq[0:m, 0, b:b + 1], xr[0:m, b, :], ALU.mult, ALU.add))
                stt(hp[0:m, b, :], bankf[0:m, o + D:o + 2 * D], ssq[0:m, 1, b:b + 1], xr[0:m, b, :],
                    ALU.mult, ALU.add).then_inc(out_used, 1)
                dve.wait_ge(out_used, b + 1)
                for x in range(2):
                    last = nc.vector.bn_stats(stats[0:m, 6 * x:6 * x + 6], hp[0:m, b, x * 512:x * 512 + 512])
                link(last)
                link(nc.vector.bn_aggr(mv[0:m, b, :], stats[0:m, :]))
            tsc(rstd[:, :], mv[:, :, 1], EPS, None, ALU.add).then_inc(var_ready, 1)
            dve.wait_ge(ln_root, 1)
            link(nc.vector.reciprocal(rstd[:, :], rstd[:, :]))
            for b in range(BLOCKS):
                _, m = bytes_of_blocks(b)
                link(tsc(hp[0:m, b, :], hp[0:m, b, :], mv[0:m, b, 0:1], rstd[0:m, b:b + 1], ALU.subtract, ALU.mult))
                link(tt(hp[0:m, b, :], hp[0:m, b, :], rows1[0:m, 1, :], ALU.mult))
                tt(hS[0:m, b, :], hp[0:m, b, :], rows1[0:m, 2, :], ALU.add).then_inc(h_ready, 1)

            for b in range(BLOCKS):
                _, m = bytes_of_blocks(b)
                dve.wait_ge(ple_full, b + 1)
                dve.wait_ge(gate_sig, b + 1)
                if b >= 2:
                    dve.wait_ge(base_out[b % 2], 16 * (b // 2))
                dve.wait_ge(h_ready, b + 1)
                tt(bout[b % 2][0:m], sgm[0:m], bankf[0:m, 4 * 512:6 * 512], ALU.mult).then_inc(ple_used, 1)
                dve.wait_ge(ple_used, b + 1)
                stt(bout[b % 2][0:m], hS[0:m, b, :], ALPHA, bout[b % 2][0:m], ALU.mult, ALU.add).then_inc(base_made, 1)

            def best16(v, i, x, m):
                link(nc.vector.max(v[:, 0:8], x))
                nc.vector.max_index(i[:, 0:8], v[:, 0:8], x)
                link(nc.vector.match_replace(sw[0:m, 0:x.shape[1]], v[:, 0:8], x, NEG))
                link(nc.vector.max(v[:, 8:16], sw[0:m, 0:x.shape[1]]))
                return nc.vector.max_index(i[:, 8:16], v[:, 8:16], sw[0:m, 0:x.shape[1]])

            def pick(b):
                _, m = bytes_of_blocks(b)
                for c in range(4):
                    dve.wait_ge(s_ready, 4 * b + c + 1)
                    for j in range(4):
                        last = best16(tv[0:m, 4 * c + j, :], ti[0:m, 4 * c + j, :], sS[0:m, c % 2, j, :], m)
                    last.then_inc(s_used, 1)
                    dve.wait_ge(s_used, 4 * b + c + 1)
                    for e in range(2):
                        h = 2 * c + e
                        a = tv[0:m, 2 * h, :].unsqueeze(2).broadcast_to([m, PK, PK])
                        d = tv[0:m, 2 * h + 1, :].unsqueeze(1).broadcast_to([m, PK, PK])
                        link(tt(cand[0:m, e, :].rearrange("p (a b) -> p a b", b=PK), a, d, ALU.add))
                        link(best16(sc[0:m, h, :], ci[0:m, h, :], cand[0:m, e, :], m))
                tt(gx[0:m], sc[0:m], sc[0:m, :, 0:1].broadcast_to([m, PH, PK]), ALU.subtract).then_inc(gx_ready, 1)
                cif = ci[0:m].rearrange("p a b -> p (a b)")
                tsc(cab[0:m, 0, :], cif, 4, None, ALU.logical_shift_right)
                tsc(cab[0:m, 1, :], cif, 15, None, ALU.bitwise_and)
                link(nc.vector.tensor_copy(tif[0:m], ti[0:m]))
                link(nc.vector.tensor_copy(cabf[0:m], cab[0:m]))
                for x in range(2):
                    for g in range(2):
                        sel = cabf[0:m, x, 64 * g:64 * g + 64].unsqueeze(2).broadcast_to([m, 64, PK])
                        link(tt(oh[0:m], sel, iota[0:m, :].unsqueeze(1).broadcast_to([m, 64, PK]), ALU.is_equal))
                        key = tif[0:m].rearrange("p (h x) a -> p h x a", x=2)[:, 4 * g:4 * g + 4, x, :]
                        o4 = oh[0:m].rearrange("p (h k) a -> p h k a", k=PK)
                        link(tt(o4, o4, key.unsqueeze(2).broadcast_to([m, 4, PK, PK]), ALU.mult))
                        link(nc.vector.tensor_reduce(e12[0:m, x, 64 * g:64 * g + 64], oh[0:m], AX.X, ALU.add))
                link(stt(efl[0:m], e12[0:m, 0, :], float(NKEY), e12[0:m, 1, :], ALU.mult, ALU.add))
                dve.wait_ge(gexp_done, b + 1)
                link(nc.vector.tensor_reduce(gsm[0:m], gx[0:m], AX.X, ALU.add))
                link(nc.vector.reciprocal(gsm[0:m], gsm[0:m]))
                gs = gsm[0:m].unsqueeze(2).broadcast_to([m, PH, PK])
                c0 = b * EXP
                if b < QB:
                    nc.vector.tensor_copy(eall[0:m, c0:c0 + EXP], efl[0:m])
                    tt(gall[0:m, c0:c0 + EXP].rearrange("p (a b) -> p a b", b=PK), gx[0:m], gs, ALU.mult).then_inc(picked, 1)
                else:
                    nc.vector.tensor_copy(eu[0:m], efl[0:m])
                    nc.vector.tensor_copy(eall[0:m, c0:c0 + 64], efl[0:m, 0:64])
                    nc.vector.memset(eall[:, STEPS:STEPS + RING].bitcast(F32), 0.0)
                    link(tt(gx[0:m], gx[0:m], gs, ALU.mult))
                    nc.vector.tensor_copy(gall[0:m, c0:c0 + 64], gx[0:m, 0:4, :].rearrange("p a b -> p (a b)")).then_inc(picked, 1)

            def dot(b):
                if b == QB:
                    dve.wait_ge(hdup, 16)
                    dve.wait_ge(packed, 32)
                dve.wait_ge(picked, b + 1)
                n_it = (EXP if b < QB else EXP // 2) // RING
                i0 = b * EXP // RING
                with dve.Fori(i0, i0 + n_it) as i:
                    for half in range(2):
                        for s in range(HALF):
                            r = half * HALF + s
                            dve.wait_ge(landed[r], 16 * i + 16)
                            last = nc.vector.tensor_tensor_reduce(
                                ring[:, r, 0:D], ring[:, r, 0:D], hS[:, b, :], 1.0, 0.0, ALU.mult, ALU.add,
                                dots[:, half, s:s + 1])
                        last.then_inc(dotted, 1)
                        dve.wait_ge(gelued, 2 * i + half + 1)
                        tt(wts[:, half, :], gel[:, half, :], gall[:, bass.ds(i * RING + half * HALF, HALF)],
                           ALU.mult).then_inc(weighed, 1)

            def norm_y(b):
                _, m = bytes_of_blocks(b)
                acc = bankf[0:m, (4 + 2 * (b % 2)) * 512:(6 + 2 * (b % 2)) * 512]
                steps = EXP * (b + 1) if b < QB else STEPS
                dve.wait_ge(slot_free, RING + steps)
                for x in range(2):
                    last = nc.vector.bn_stats(stats[0:m, 6 * x:6 * x + 6], acc[:, x * 512:x * 512 + 512])
                link(last)
                link(nc.vector.bn_aggr(lnrow[0:m, 0:2], stats[0:m, :]))
                tsc(lnrow[:, 1:2], lnrow[:, 1:2], EPS, None, ALU.add).then_inc(y_var, 1)
                dve.wait_ge(y_root, b + 1)
                link(nc.vector.reciprocal(lnrow[:, 3:4], lnrow[:, 2:3]))
                if b >= 1:
                    dve.wait_ge(ysem, 16 * b)
                tsc(ybuf[0:m], acc, lnrow[0:m, 0:1], lnrow[0:m, 3:4], ALU.subtract, ALU.mult).then_inc(acc_used, 1)
                dve.wait_ge(acc_used, b + 1)
                link(tt(ybuf[0:m], ybuf[0:m], rows2[0:m, 0, :], ALU.mult))
                tt(ybuf[0:m], ybuf[0:m], rows2[0:m, 1, :], ALU.add).then_inc(y_made, 1)

            pick(0)
            dve.wait_ge(in_rows2, 16)
            for b in range(BLOCKS):
                if b + 1 < BLOCKS:
                    pick(b + 1)
                dot(b)
                norm_y(b)


def multiplicity(d):
    return sum(((d >= 0) & (d <= w) & (d % s == 0)).astype(np.float64) for w, s in BRANCHES)


def bias_of(d, slope):
    m = multiplicity(d)
    return np.where(m > 0, -slope * d + np.log(np.maximum(m, 1)), -1.0e30).astype(np.float32)


def tiles(w, parts):
    k, n = w.shape
    return np.ascontiguousarray(w.reshape(k // P, P, parts, n // parts).transpose(2, 1, 0, 3).reshape(parts, P, -1))


def by_channel(v):
    return v.reshape(-1, P).T


def spread(v):
    return np.broadcast_to(v, (P,) + v.shape)


def cache_order():
    r = np.arange(PAST)
    old = r < PAST - 512
    return np.concatenate([r[old & (r % 16 < NT)], r[~old], r[old & (r % 16 >= NT)]])


def layouts(i):
    sq = {k: np.asarray(v) for k, v in i.items()}
    x = np.concatenate([sq["x_prompt"].reshape(SEQ, D), sq["x_sample"].reshape(ST, D)])
    p = np.concatenate([sq["p_prompt"].reshape(SEQ, PLE), sq["p_sample"].reshape(ST, PLE)])
    order = cache_order()
    b_in = sq["b_in"][0]
    a = {"x_rows": x, "xT": x.T.reshape(DC, P, TOK).transpose(1, 0, 2),
         "pT": p.T.reshape(2, P, TOK).transpose(1, 0, 2)}
    a["w_in"] = tiles(sq["w_in"][0], 4)
    a["w_out"] = tiles(sq["w_out"][0], 2)
    a["w_gate"] = tiles(sq["w_ple_gate"][0], 2)
    a["w_pq"] = tiles(sq["w_pq"][0], 4)
    a["glu_ple"] = np.concatenate([tiles(sq["w_glu"][0], 1)[0], tiles(sq["w_ple"][0], 1)[0]], axis=1)
    a["vrow"] = spread(b_in[2 * AW:3 * AW])
    a["cols"] = np.concatenate(
        [by_channel(b_in[0:AW]), by_channel(b_in[AW:2 * AW]), by_channel(b_in[3 * AW:])]
        + [by_channel(sq[n][0].reshape(-1)) for n in ("b_glu", "g_att_out", "g_ssm_out", "ssm_d")], axis=1)
    a["rows1"] = spread(np.stack([sq["b_out"][0], sq["ln1_g"][0], sq["ln1_b"][0]]))
    a["rows2"] = spread(np.stack([sq["ln2_g"][0], sq["ln2_b"][0]]))

    def states(v):
        return v.reshape(SJ, P).T

    dt = np.broadcast_to(sq["log_dt"][0][:, None], (NG, NS))
    a["lam"] = np.stack([states(sq["lam_re"][0]), states(sq["lam_im"][0]), states(dt)], axis=1)
    bt = np.zeros((4, 2, GC, CT, 4, 2, 2, NS), np.float32)
    ct = np.zeros((2, NS, SJ, 2, 2, GC), np.float32)
    for x, (bn, cn) in enumerate((("ssm_b_re", "ssm_c_re"), ("ssm_b_im", "ssm_c_im"))):
        bg = sq[bn][0].reshape(CT, 4, 2, NS, GC)
        cg = sq[cn][0].reshape(SJ, 2, GC, NS)
        for g in range(2):
            for j in range(4):
                bt[j, g, :, :, j, x, g, :] = bg[:, j, g].transpose(2, 0, 1)
            ct[g, :, :, x, g, :] = cg[:, g].transpose(2, 0, 1)
    a["Bt"] = bt.reshape(P, SJ, 2, P)
    a["Ct"] = ct.reshape(P, SJ, 2, 32)
    a["h0"] = np.stack([sq[n][0].reshape(NB, SJ, P).transpose(2, 1, 0) for n in ("state_ssm_re", "state_ssm_im")], axis=1)
    kc = sq["cache_k"][0].reshape(NB, PAST, AW)[:, order]
    vc = sq["cache_v"][0].reshape(NB, PAST, AW)[:, order]
    a["kc"] = kc.transpose(0, 2, 1).reshape(NB, CT, P, PAST).transpose(0, 2, 1, 3)
    a["vc"] = vc.reshape(NB, PAST // P, P, AW).transpose(0, 2, 1, 3)
    a["keysT"] = np.stack([sq["sub_keys1"][0].T, sq["sub_keys2"][0].T], axis=1)
    a["uv"] = np.concatenate([sq["peer_u"][0], sq["peer_v"][0]], axis=1)

    slopes = 2.0 ** (-8.0 * np.arange(1, NH + 1) / NH)
    d = np.arange(P)[:, None] - np.arange(SEQ)[None, :] + (SEQ - P)
    a["pbias"] = np.stack([bias_of(d, s) for s in slopes], axis=1)
    t = np.arange(NT)
    cache_d = PAST + t[:, None] - order[None, :NK]
    own = t[:, None] - t[None, :]
    sb = np.full((NH, NT, NK + NB * ST), -1.0e30, np.float32)
    for h, s in enumerate(slopes):
        sb[h, :, :NK] = bias_of(cache_d, s)
        for b in range(NB):
            sb[h, :, NK + b * ST + b * NT:NK + b * ST + (b + 1) * NT] = bias_of(own, s)
    a["sbias"] = sb.reshape(ST, -1)
    a["ident"] = np.eye(P, dtype=np.float32)
    a["fold"] = np.tile(np.eye(ST, dtype=np.float32), (2, 1))
    a["iota"] = spread(np.arange(PK, dtype=np.float32))
    return {k: np.ascontiguousarray(v) for k, v in a.items()}


def kernel(**inputs):
    import concourse.bacc as bacc
    from concourse.bass_utils import run_bass_kernel_spmd as run

    nc = bacc.Bacc("TRN2", target_bir_lowering=False, num_devices=1)
    arrays = layouts(inputs)
    A = {n: nc.dram_tensor("d_" + n, v.shape, mybir.dt.from_np(v.dtype), kind="ExternalInput").ap() for n, v in arrays.items()}
    made = {"y": (TOK, D), "k_out": (P, CT, TOK), "v_out": (TOK, AW), "stp_out": (P, 2, SJ), "sts_out": (P, 2, SJ, NB)}
    for n, shape in made.items():
        A[n] = nc.dram_tensor("d_" + n, shape, F32, kind="ExternalOutput").ap()
    A["base"] = nc.dram_tensor("d_base", (TOK, D), F32, kind="Internal").ap()
    build(nc, A)
    r = run(nc, [{"d_" + n: v for n, v in arrays.items()}], core_ids=[0]).results[0]
    r = {n: r["d_" + n] for n in made}
    y, v = r["y"], r["v_out"]
    k = r["k_out"].transpose(1, 0, 2).reshape(AW, TOK).T
    stp = r["stp_out"].transpose(1, 2, 0).reshape(2, 1, 1, NG, NS)
    sts = r["sts_out"].transpose(1, 3, 2, 0).reshape(2, 1, NB, NG, NS)
    return (y[:SEQ].reshape(1, SEQ, D), y[SEQ:].reshape(NB, NT, D),
            k[:SEQ].reshape(1, 1, SEQ, NH, HD), v[:SEQ].reshape(1, 1, SEQ, NH, HD),
            stp[0], stp[1],
            k[SEQ:].reshape(1, NB, NT, NH, HD), v[SEQ:].reshape(1, NB, NT, NH, HD),
            sts[0], sts[1])
```

```python
from contextlib import ExitStack

import numpy as np
import concourse.bass as bass
from concourse import mybir

F32 = mybir.dt.float32
U32 = mybir.dt.uint32
ALU = mybir.AluOpType
ACT = mybir.ActivationFunctionType
AX = mybir.AxisListType

P = 128
D = 1024
DC = D // P
AW = 512
CT = AW // P
NH, HD = 8, 64
SEQ, NB, NT = 512, 8, 8
ST = NB * NT
TOK = SEQ + ST
QB = SEQ // P
BLOCKS = QB + 1
PAST = 2048
BRANCHES = ((128, 1), (512, 4), (2048, 16))
NG, GC, NS = 32, 16, 64
SJ = NG * NS // P
COLD = (PAST - 512) // 2
NK = COLD + 512
KT = NK // P
SK = NK + ST
PLE = 256
PH, PK = 8, 16
EXP = PH * PK
NKEY = 128
ALPHA = 2.0 ** 0.25
EPS = 1e-5
RING = 8
HALF = RING // 2
PAIR = 2
STEPS = QB * EXP + EXP // 2
TWO_PI = 2.0 * np.pi
TP_HI = 6.28125
TP_LO = TWO_PI - TP_HI
FIRST_BANKS = 1024
WIDE = TOK // 2
ROUND = 1.5 * 2.0 ** 23
NEG = -3.0e38


def column(i, at, n):
    return slice(i * RING + at, i * RING + at + n) if isinstance(i, int) else bass.ds(i * RING + at, n)


def block_of(half_turn):
    return half_turn * HALF // EXP


def turns(engine, h0, h1, half_turn):
    if h0 % 2 and h0 < h1:
        half_turn(h0 // 2, 1)
        h0 += 1
    if h1 - h0 >= 4:
        with engine.Fori(h0 // 2, h1 // 2) as i:
            for x in range(2):
                half_turn(i, x)
        h0 = h1 // 2 * 2
    for h in range(h0, h1):
        half_turn(h // 2, h % 2)


def tokens_of(b):
    return b * P, (P if b < QB else ST)


def k_turn(b):
    return 2 * b - (b > 0)


def v_turn(b):
    return 2 * b + 2 - (b == NB - 1)


CACHE_TURNS = sorted([("k", b) for b in range(NB)] + [("v", b) for b in range(NB)],
                     key=lambda x: k_turn(x[1]) if x[0] == "k" else v_turn(x[1]))

PART_SLOT = [3, 0, 1, 2]

OUT_BANK = [0, 4, 4, 0, 4]

GLU_BEFORE = {NB - 3: 0, NB - 2: 2}
GLU_AFTER = {NB - 3: 1, NB - 2: 3}
SSM_OUT_AT = NB - 4


def order_of_work():
    picks = [(b, c) for b in range(BLOCKS) for c in range(4)]
    order = []
    turn = 0

    block = 2 * EXP // RING

    def experts(halves):
        nonlocal turn
        end = turn + halves
        while turn < end:
            upto = min(end, (turn // block + 1) * block)
            order.append(("experts", turn, upto))
            turn = upto

    for n in range(1, len(picks)):
        coming = picks[n + 1:n + 2]
        experts(1)
        order += [("ask", *x) for x in coming]
        order.append(("tops", *picks[n], 0))
        experts(1)
        order += [("ask_out", *x) for x in coming]
        order.append(("tops", *picks[n], 1))
        experts(1)
        order += [("match", *x) for x in coming]
        order.append(("cross", *picks[n]))
        experts(1)
        order += [("match_out", *x) for x in coming]
        order += [("turn", b) for b, c in picks[n + 2:n + 3] if c == 0]
        order.append(("resolve", *picks[n]))
        if turn == block:
            order.append(("put_by", 0))

    def gate(b):
        experts(1)
        order.append(("gate_turn", b))
        experts(2)
        for half in range(2):
            order.append(("gate", b, half))
            experts(1)
            order.append(("gate_out", b, half))
            experts(2 if b < 2 else 3)

    for b in range(3):
        gate(b)
        order.append(("finish", b))
    gate(3)
    gate(4)
    experts(4 * block + 2 - turn)
    order.append(("finish", 3))
    experts(2 * STEPS // RING - turn)
    return order + [("finish", 4)]


ORDER = order_of_work()


def build(nc, A):
    ctx = ExitStack()
    with ctx:
        def sb(name, shape, dt=F32):
            return ctx.enter_context(nc.sbuf_tensor(name, shape, dt))

        def sem(name):
            return ctx.enter_context(nc.semaphore(name))

        W = sb("W", [P, 4, 4096])
        R = sb("R", [P, 16384])
        E = sb("E", [P, 19456])
        Wf = W[:, :, :].rearrange("p a b -> p (a b)")

        def view(base, at, *dims):
            n = int(np.prod(dims))
            v = base[:, at:at + n]
            if len(dims) == 2:
                v = v.rearrange("p (a b) -> p a b", a=dims[0])
            if len(dims) == 3:
                v = v.rearrange("p (a b c) -> p a b c", a=dims[0], b=dims[1])
            return v

        ident = sb("ident", [P, P])
        fold = sb("fold", [P, ST])
        iota = sb("iota", [P, PK])
        ones = sb("ones", [P, 2])
        cols = sb("cols", [P, 28])
        ssq = sb("ssq", [P, 2, BLOCKS])
        mv = sb("mv", [P, BLOCKS, 2])
        rstd = sb("rstd", [P, BLOCKS])
        stats = sb("stats", [P, 12])
        lnrow = sb("lnrow", [P, 4])
        lam = sb("lam", [P, 3, SJ])
        sm = sb("sm", [P, 20, SJ])
        small = sb("small", [P, 16])

        xT = view(E, 0, DC, TOK)
        mixT = xT
        qT = view(E, 4608, CT, TOK)
        kT = view(E, 6912, CT, TOK)
        uT = view(E, 9216, CT, TOK)
        vS = view(E, 11520, BLOCKS, AW)
        zT = view(E, 14080, CT, TOK)
        Craw = view(E, 17408, SJ, 2, 32)
        Csc = view(E, 18432, SJ, 2, 32)
        hS = view(E, 4608, BLOCKS, D)
        hT = view(E, 9728, DC, P)
        ybuf = view(E, 10752, D)
        qpT = view(E, 11776, 2, 512)
        sS = view(E, 12800, 2, 4, NKEY)
        sw = view(E, 13824, 256)
        cand = view(E, 14080, 2, 256)
        oh = view(E, 14592, 2 * PK, PK)
        gall = view(E, 15616, STEPS + RING)
        eall = view(E, 16208, STEPS + RING).bitcast(U32)
        tv = view(E, 16800, 4, PK)
        ti = view(E, 16864, 4, PK).bitcast(U32)
        tif = view(E, 16928, 4, PK)
        sc = view(E, 16992, 2, PK)
        ci = view(E, 17024, 2, PK).bitcast(U32)
        cab = view(E, 17056, 2, 2 * PK).bitcast(U32)
        cabf = view(E, 17120, 2, 2 * PK)
        e12 = view(E, 17184, 2, 2 * PK)
        efl = view(E, 17248, 2 * PK)
        gx = view(E, 17280, 2, PK)
        gsm = view(E, 17312, 2)
        up_e = view(E, 17316, 4 * PK).bitcast(U32)
        up_g = view(E, 17380, 4 * PK)
        dots = view(E, 19008, 2, HALF)
        gel = view(E, 19016, 2, HALF)
        wts = view(E, 19024, 2, HALF)
        stage = view(E, 19032, 2, HALF).bitcast(U32)
        diag = view(E, 0, RING, P)
        rows2 = view(E, 1024, 2, D)
        keep = view(E, 3072, D)
        alpha_id = view(E, 4096, P)
        keysT = view(E, 19040, 2, NKEY)

        pbias = view(R, 0, NH, SEQ)
        tc = view(R, 5120, SJ, P)
        ts = view(R, 7168, SJ, P)
        tm = view(R, 9216, SJ, P)
        wt = [view(R, 11264 + 1024 * i, 1024) for i in range(4)]
        rr = [view(R, 11264 + 512 * i, 4, P) for i in range(6)]
        turned = [[view(R, 14336 + 512 * c, 4, P) for c in range(4)],
                  [view(Wf, 8960 + 512 * c, 4, P) for c in range(4)]]
        Cneg = view(Wf, 11008, SJ, 32)
        vrow = view(R, 4096, AW)
        poolt1 = view(R, 15360, SJ, ST)
        kcS = [view(R, 5120 * n, CT, NK) for n in range(3)]
        vcS = [view(R, 5120 * n, KT, AW) for n in range(3)]
        rows1 = view(R, 5120 * (v_turn(NB - 1) % 3), 3, D)
        wout = [view(R, 5120 * (k_turn(NB - 1) % 3), DC, 512), view(R, 5120 * (v_turn(NB - 2) % 3), DC, 512)]
        ring = [view(R, 2 * D * ((r + 2) % RING), 2 * D) for r in range(RING)]

        pbuf = view(Wf, 0, 2, SK)
        ptS = view(Wf, 2688, 2, KT * ST + ST)
        atok = view(Wf, 4096, 2, AW)
        qblk = view(Wf, 5120, NB, CT, ST)
        sbias = view(Wf, 7168, NK + NB * ST)
        xs = [view(Wf, 8960 + 1024 * i, SJ, ST) for i in range(2)]
        poolt2 = view(Wf, 11008, SJ, ST)
        oS = view(Wf, 4096, P)
        sq = view(Wf, 8960, CT, TOK)
        sg = [view(Wf, 11264, TOK), view(R, 15360, TOK)]
        Bt = Wf[:, 3 * 4096:4 * 4096].rearrange("p (j x n) -> p j x n", j=SJ, x=2)
        glu = view(Wf, 3 * 4096, CT, 512)
        ple = view(Wf, 2 * 4096, 2, D)
        pT = view(Wf, 2 * 4096 + 2048, 2, TOK)
        sgm = view(Wf, 2 * 4096 + 3200, 512)
        gp = view(Wf, 3 * 4096, 4, D)
        asc = view(Wf, 12032, CT, ST)
        h0 = sb("h0", [P, 2, SJ, NB])
        xs_last = [h0[:, c] for c in range(2)]

        bank = ctx.enter_context(nc.psum_tensor("bank", [P, 8, 512], F32))
        bankf = bank[:, :, :].rearrange("p a b -> p (a b)")

        in_x = [sem("in_x0"), sem("in_x1")]
        in_lam, in_cols, in_const, in_ssm, in_pb, in_vrow = (
            sem(n) for n in ("in_lam", "in_cols", "in_const", "in_ssm", "in_pb", "in_vrow"))
        in_w = [sem(f"in_w{i}") for i in range(4)]
        in_Bt, in_sb, in_glu = sem("in_Bt"), sem("in_sb"), sem("in_glu")
        in_cache = [sem(f"in_cache{i}") for i in range(3)]
        in_w_first = sem("in_w_first")
        in_rows1, in_xr = sem("in_rows1"), sem("in_xr")
        in_out = [sem(f"in_out{i}") for i in range(2)]
        in_gate, in_rows2, in_keys = sem("in_gate"), sem("in_rows2"), sem("in_keys")
        in_pq = [sem(f"in_pq{i}") for i in range(4)]
        ysem, outs, kv_left = sem("ysem"), sem("outs"), sem("kv_left")
        os_zero, so_copied, so_turned = sem("os_zero"), sem("so_copied"), sem("so_turned")
        proj_full = sem("proj_full")
        q_done, k_done, v_done, u_done = (sem(n) for n in ("q_done", "k_done", "v_done", "u_done"))
        dve_chain, act_chain, pool_chain = sem("dve_chain"), sem("act_chain"), sem("pool_chain")
        trig_arg, trig_done, exp_done = sem("trig_arg"), sem("trig_done"), sem("exp_done")
        ssm_exp_in = sem("ssm_exp_in")
        tables_done = sem("tables_done")
        sc_full, sc_biased, p_ready, p_turned, pt_ready, o_full, o_normed, inverted = (
            sem(n) for n in ("sc_full", "sc_biased", "p_ready", "p_turned", "pt_ready", "o_full", "o_normed",
                             "inverted"))
        at_full, at_done = sem("at_full"), sem("at_done")
        bu_full, bu_used, hs_ready, y_full, y_used = (
            sem(n) for n in ("bu_full", "bu_used", "hs_ready", "y_full", "y_used"))
        ones_set, qblk_zero, qblk_set = sem("ones_set"), sem("qblk_zero"), sem("qblk_set")
        sbu_full, sbu_used, sx_ready, sy_full, sy_used = (
            sem(n) for n in ("sbu_full", "sbu_used", "sx_ready", "sy_full", "sy_used"))
        ss_full, ss_biased, sp_exp, sp_ready, sp_turned, spt_ready, so_full, so_used = (
            sem(n) for n in ("ss_full", "ss_biased", "sp_exp", "sp_ready", "sp_turned", "spt_ready", "so_full", "so_used"))
        z_ready, glu_full, sig_ready, mixed, sq_full, ssq_ready, rms_root = (
            sem(n) for n in ("z_ready", "glu_full", "sig_ready", "mixed", "sq_full", "ssq_ready", "rms_root"))
        out_full, out_used, var_ready, ln_root, h_ready = (
            sem(n) for n in ("out_full", "out_used", "var_ready", "ln_root", "h_ready"))
        ht_full, ht_ready, gate_full, gate_sig, gate_used = (
            sem(n) for n in ("ht_full", "ht_ready", "gate_full", "gate_sig", "gate_used"))
        cneg_set, ss_first, carried = sem("cneg_set"), sem("ss_first"), sem("carried")
        alpha_set, asc_ready = sem("alpha_set"), sem("asc_ready")
        pq_full, pq_ready, s_full, s_ready, s_used = (
            sem(n) for n in ("pq_full", "pq_ready", "s_full", "s_ready", "s_used"))
        gx_ready, gexp_done, picked, packed = (sem(n) for n in ("gx_ready", "gexp_done", "picked", "packed"))
        hdup = sem("hdup")
        staged, granted, slot_free, dotted, gelued, weighed, diagonal = (
            sem(n) for n in ("staged", "granted", "slot_free", "dotted", "gelued", "weighed", "diagonal"))
        landed = [sem(f"landed{r}") for r in range(RING)]
        y_var, y_root, y_made = sem("y_var"), sem("y_root"), sem("y_made")
        acc_used = sem("acc_used")

        PROJ = ([("q", c) for c in range(CT)] + [("k", c) for c in range(CT)]
                + [("v", b) for b in range(BLOCKS)] + [("u", c) for c in range(CT)])
        UNITS = [(qb, h) for qb in range(QB) for h in range(NH)]

        block = ctx.enter_context(nc.Block())

        @block.sync
        def _(sp):
            def load(dst, src, s):
                sp.dma_start(dst, src).then_inc(s, 16)

            def columns(w, c0, c1):
                return w.rearrange("p (c n) -> p c n", c=DC)[:, :, c0:c1]

            load(columns(W[:, PART_SLOT[0], :], 0, P), columns(A["w_in"][0], 0, P), in_w_first)
            for x in range(2):
                load(xT[:, :, x * WIDE:(x + 1) * WIDE], A["xT"][:, :, x * WIDE:(x + 1) * WIDE], in_x[x])
            load(lam[:, :, :], A["lam"], in_lam)
            load(cols[:, :], A["cols"], in_cols)
            load(columns(W[:, PART_SLOT[0], :], P, 512), columns(A["w_in"][0], P, 512), in_w[0])
            load(W[:, PART_SLOT[1], :], A["w_in"][1], in_w[1])
            load(ident[:, :], A["ident"], in_const)
            load(fold[:, :], A["fold"], in_const)
            load(iota[:, :], A["iota"], in_const)
            load(vrow, A["vrow"], in_vrow)
            load(W[:, PART_SLOT[2], :], A["w_in"][2], in_w[2])
            load(Craw, A["Ct"], in_ssm)
            load(h0[:, :, :, :], A["h0"], in_ssm)
            load(W[:, PART_SLOT[3], :], A["w_in"][3], in_w[3])
            load(pbias, A["pbias"], in_pb)
            sp.wait_ge(proj_full, CT)
            load(Bt, A["Bt"], in_Bt)
            sp.wait_ge(v_done, BLOCKS)
            for b in range(BLOCKS):
                t0, n = tokens_of(b)
                sp.dma_start(A["v_out"][t0:t0 + n, :], vS[0:n, b, :]).then_inc(kv_left, 16)
            sp.wait_ge(k_done, CT)
            sp.dma_start(A["k_out"], kT).then_inc(kv_left, 16)
            sp.wait_ge(proj_full, len(PROJ))
            load(sbias[0:ST], A["sbias"], in_sb)
            sp.wait_ge(sc_biased, len(UNITS))
            for n, (kind, b) in enumerate(CACHE_TURNS):
                if n == 1:
                    sp.wait_ge(y_used, 4 * QB)
                    sp.wait_ge(carried, 4 * QB)
                if n >= 3:
                    what, b0 = CACHE_TURNS[n - 3]
                    sp.wait_ge(ss_full if what == "k" else so_full, b0 + 1)
                if kind == "k":
                    load(kcS[n % 3], A["kc"][b][:, :, 0:NK], in_cache[n % 3])
                else:
                    load(vcS[n % 3], A["vc"][b][:, 0:KT, :], in_cache[n % 3])
                if n == 5:
                    sp.wait_ge(sbu_full, 2)
                    load(glu, A["glu"], in_glu)
            sp.wait_ge(ss_full, NB)
            load(wout[0], A["w_out"][0].rearrange("p (c n) -> p c n", c=DC), in_out[0])
            sp.wait_ge(so_full, NB - 1)
            load(wout[1], A["w_out"][1].rearrange("p (c n) -> p c n", c=DC), in_out[1])
            sp.wait_ge(glu_full, CT)
            load(W[:, 3, :], A["w_pq"][0], in_pq[0])
            sp.wait_ge(kv_left, 16 * (BLOCKS + 1))
            sp.wait_ge(qblk_set, 1)
            sp.wait_ge(sy_used, 1)
            for b in range(BLOCKS):
                t0, n = tokens_of(b)
                load(hS[0:n, b, :], A["x_rows"][t0:t0 + n, :], in_xr)
            load(keysT, A["keysT"], in_keys)
            sp.wait_ge(so_full, NB)
            load(rows1, A["rows1"], in_rows1)
            load(W[:, 0, :], A["w_pq"][1], in_pq[1])
            sp.wait_ge(so_turned, NB)
            load(W[:, 1, :], A["w_pq"][2], in_pq[2])
            sp.wait_ge(sq_full, 1)
            load(W[:, 2, :], A["w_pq"][3], in_pq[3])
            sp.wait_ge(out_full, BLOCKS)
            load(rows2, A["rows2"], in_rows2)
            sp.wait_ge(carried, 4 * QB)
            sp.dma_start(A["stp_out"], sm[:, 14:16, :]).then_inc(outs, 16)
            for c in range(2):
                sp.dma_start(A["sts_out"][:, c], xs_last[c]).then_inc(outs, 16)
            sp.wait_ge(h_ready, BLOCKS)
            sp.dma_start(hS[ST:P, QB, :], hS[0:ST, QB, :]).then_inc(hdup, 16)
            sp.wait_ge(picked, 4 * BLOCKS)
            c0 = QB * EXP
            sp.dma_start(eall[ST:P, c0:c0 + 64], up_e[0:ST]).then_inc(packed, 16)
            sp.dma_start(gall[ST:P, c0:c0 + 64], up_g[0:ST]).then_inc(packed, 16)
            sp.wait_ge(pq_full, 4 * BLOCKS)
            load(W[:, 0, :], A["w_gate"][0], in_gate)
            load(W[:, 1, :], A["w_gate"][1], in_gate)
            load(ple, A["w_ple"], in_gate)
            load(pT, A["pT"], in_gate)
            for b in range(BLOCKS):
                t0, m = tokens_of(b)
                sp.wait_ge(y_made, b + 1)
                sp.dma_start(A["y"][t0:t0 + m, :], ybuf[0:m]).then_inc(ysem, 16)
            sp.wait_ge(ysem, 16 * BLOCKS)
            sp.wait_ge(outs, 16 * 3)

        @block.gpsimd
        def _(pool):
            n_link = [0]

            def link(ins):
                n_link[0] += 1
                ins.then_inc(pool_chain, 1)
                pool.wait_ge(pool_chain, n_link[0])

            tt = nc.gpsimd.tensor_tensor
            nc.gpsimd.memset(ones[:, :], 1.0).then_inc(ones_set, 1)
            pool.wait_ge(proj_full, len(PROJ))
            nc.gpsimd.memset(qblk.rearrange("p a b c -> p (a b c)"), 0.0).then_inc(qblk_zero, 1)

            def wide(k, n):
                return sm[:, k, :].unsqueeze(2).broadcast_to([P, SJ, n])

            for n in range(4 * QB):
                b, q = divmod(n, 4)
                j = slice(4 * q, 4 * q + 4)
                k, o = (0, 16) if b < QB - 1 else (10, 14)
                p_rc, p_is, p_rs, p_ic = (x[:, :, P - 1] for x in turned[n % 2])
                hl, hi = sm[:, 7, j], sm[:, 8, j]
                pool.wait_ge(hs_ready, n + 1)
                tt(hl, p_rc, p_is, ALU.subtract)
                link(tt(hi, p_rs, p_ic, ALU.add))
                tt(sm[:, 18, j], hl, sm[:, k, j], ALU.mult)
                tt(sm[:, 19, j], hi, sm[:, k + 1, j], ALU.mult)
                tt(sm[:, 12, j], hl, sm[:, k + 1, j], ALU.mult)
                link(tt(sm[:, 13, j], hi, sm[:, k, j], ALU.mult))
                tt(sm[:, o, j], sm[:, 18, j], sm[:, 19, j], ALU.subtract)
                tt(sm[:, o + 1, j], sm[:, 12, j], sm[:, 13, j], ALU.add).then_inc(carried, 1)

            pool.wait_ge(at_done, QB)
            nc.gpsimd.memset(oS, 0.0).then_inc(os_zero, 1)
            pool.wait_ge(tables_done, 1)
            pool.wait_ge(sbu_used, 2)
            link(tt(poolt1, xs[0], wide(10, ST), ALU.mult))
            link(tt(poolt2, xs[1], wide(11, ST), ALU.mult))
            link(tt(poolt1, poolt1, poolt2, ALU.subtract))
            link(tt(poolt2, xs[1], wide(10, ST), ALU.mult))
            link(tt(xs[1], xs[0], wide(11, ST), ALU.mult))
            link(tt(xs[1], xs[1], poolt2, ALU.add))
            link(nc.gpsimd.tensor_copy(xs[0], poolt1))
            vr, vi = (x.rearrange("p j (b t) -> p j b t", t=NT) for x in xs)
            u1, u2 = (x.rearrange("p j (a b) -> p a j b", b=NB) for x in (poolt1, poolt2))
            for t in range(NT):
                pr = h0[:, 0, :, :] if t == 0 else vr[:, :, :, t - 1]
                pi = h0[:, 1, :, :] if t == 0 else vi[:, :, :, t - 1]
                tt(u1[:, 0], pr, wide(0, NB), ALU.mult)
                tt(u1[:, 1], pi, wide(1, NB), ALU.mult)
                tt(u2[:, 0], pi, wide(0, NB), ALU.mult)
                link(tt(u2[:, 1], pr, wide(1, NB), ALU.mult))
                tt(vr[:, :, :, t], vr[:, :, :, t], u1[:, 0], ALU.add)
                link(tt(vi[:, :, :, t], vi[:, :, :, t], u2[:, 0], ALU.add))
                tt(vr[:, :, :, t], vr[:, :, :, t], u1[:, 1], ALU.subtract)
                link(tt(vi[:, :, :, t], vi[:, :, :, t], u2[:, 1], ALU.add))
            nc.gpsimd.tensor_copy(xs_last[0], vr[:, :, :, NT - 1])
            nc.gpsimd.tensor_copy(xs_last[1], vi[:, :, :, NT - 1]).then_inc(sx_ready, 1)

            pool.wait_ge(out_full, BLOCKS)
            with pool.Fori(0, STEPS // RING) as i:
                for half in range(2):
                    pool.wait_ge(staged, 2 * i + half + 1)
                    for s in range(HALF):
                        r = half * HALF + s
                        pool.wait_ge(slot_free, i * RING + (r + 1))
                        pool.sem_inc(granted, 1)
                        pool.indirect_dma_start(
                            ring[r], None, A["uv"],
                            bass.IndirectOffsetOnAxis(ap=stage[:, half, s:s + 1], axis=0),
                        ).then_inc(landed[r], 16)

        @block.tensor
        def _(pe):
            mm = nc.tensor.matmul

            def wait_used(n):
                kind, c = PROJ[n]
                pe.wait_ge({"q": q_done, "k": k_done, "v": v_done, "u": u_done}[kind], c + 1)

            for n, (kind, c) in enumerate(PROJ):
                part = "qkvu".index(kind)
                if n == 0:
                    pe.wait_ge(in_w_first, 16)
                elif n == 1:
                    pe.wait_ge(in_w[0], 16)
                elif c == 0:
                    pe.wait_ge(in_w[part], 16)
                if n >= 2:
                    wait_used(n - 2)
                a = bank[:, 2 * (n % 2), :]
                w = W[:, PART_SLOT[part], :].rearrange("p (c n) -> p c n", c=DC)
                if kind == "v":
                    t0, m = tokens_of(c)
                    for k in range(DC):
                        last = mm(a[0:m], xT[:, k, t0:t0 + m], w[:, k, :], start=(k == 0), stop=(k == DC - 1))
                else:
                    for x in range(2):
                        if n == 0:
                            pe.wait_ge(in_x[x], 16)
                        for k in range(DC):
                            last = mm(bank[:, 2 * (n % 2) + x, 0:WIDE], w[:, k, c * P:c * P + P],
                                      xT[:, k, x * WIDE:(x + 1) * WIDE], start=(k == 0), stop=(k == DC - 1))
                last.then_inc(proj_full, 1)

            def scores(i):
                qb, h = UNITS[i]
                p0, c = 64 * (h % 2), h // 2
                if i >= 2:
                    pe.wait_ge(sc_biased, i - 1)
                mm(bank[:, i % 2, 0:P * (qb + 1)], qT[p0:p0 + 64, c, qb * P:qb * P + P],
                   kT[p0:p0 + 64, c, 0:P * (qb + 1)], start=True, stop=True).then_inc(sc_full, 1)

            def turn_probs(i):
                qb, _ = UNITS[i]
                pe.wait_ge(p_ready, i + 1)
                if i >= 2:
                    pe.wait_ge(pt_ready, i - 1)
                for k in range(qb + 1):
                    last = nc.tensor.transpose(bank[:, 2 + i % 2, k * P:k * P + P],
                                               pbuf[:, i % 2, k * P:k * P + P], ident[:, :])
                last.then_inc(p_turned, 1)

            def values(i):
                qb, h = UNITS[i]
                pe.wait_ge(pt_ready, i + 1)
                if i >= 1:
                    pe.wait_ge(o_normed, i)
                o = bank[:, 4, 0:HD]
                for k in range(qb + 1):
                    last = mm(o, ptS[:, i % 2, k * P:k * P + P], vS[:, k, h * HD:h * HD + HD],
                              start=(k == 0), stop=(k == qb))
                last.then_inc(o_full, 1)

            def turn_att(qb):
                pe.wait_ge(o_normed, NH * (qb + 1))
                pe.wait_ge(y_used, 4 * (qb + 1))
                for c in range(CT):
                    last = nc.tensor.transpose(bank[:, 5, c * P:c * P + P],
                                               atok[:, qb % 2, c * P:c * P + P], ident[:, :])
                last.then_inc(at_full, 1)

            def ssm_in(n):
                b, q = divmod(n, 4)
                if n >= 1:
                    pe.wait_ge(bu_used, n)
                for x in range(2):
                    for j in range(4):
                        last = mm(bank[:, 6 + x, j * P:j * P + P], Bt[:, 4 * q + j, x, :],
                                  uT[:, q, b * P:b * P + P], start=True, stop=True)
                last.then_inc(bu_full, 1)

            def ssm_out(n):
                q = n % 4
                pe.wait_ge(hs_ready, n + 1)
                if n >= 1:
                    pe.wait_ge(y_used, n)
                if n >= 4 and n % 4 == 0:
                    pe.wait_ge(at_done, n // 4)
                for j in range(4):
                    t = 4 * q + j
                    for x, c in enumerate((Csc[:, t, 0, :], Cneg[:, t, :], Csc[:, t, 1, :], Csc[:, t, 1, :])):
                        last = mm(bank[32 * j:32 * j + 32, 5, 0:P], c, turned[n % 2][x][:, j, :],
                                  start=(x == 0), stop=(x == 3), skip_group_check=True)
                last.then_inc(y_full, 1)

            pe.wait_ge(q_done, CT)
            pe.wait_ge(k_done, CT)
            pe.wait_ge(v_done, BLOCKS)
            pe.wait_ge(u_done, CT)
            pe.wait_ge(in_const, 16 * 3)
            pe.wait_ge(in_Bt, 16)
            pe.wait_ge(cneg_set, 1)
            scores(0)
            ssm_in(0)
            for i in range(len(UNITS) + 3):
                if i + 1 < len(UNITS):
                    scores(i + 1)
                if i < len(UNITS):
                    turn_probs(i)
                if 1 <= i <= len(UNITS):
                    values(i - 1)
                if i % 2 == 1 and i // 2 + 1 < 4 * QB:
                    ssm_in(i // 2 + 1)
                if i % 2 == 1 and 1 <= i // 2 <= 4 * QB:
                    ssm_out(i // 2 - 1)
                if i > 2 and (i - 2) % NH == 0:
                    turn_att((i - 2) // NH - 1)

            def s_ssm_in(x):
                if x == 0:
                    pe.wait_ge(y_used, 4 * QB)
                else:
                    pe.wait_ge(sbu_used, 1)
                for j in range(SJ):
                    last = mm(bankf[:, 6 * 512 + j * ST:6 * 512 + (j + 1) * ST], Bt[:, j, x, :],
                              uT[:, j // 4, SEQ:TOK], start=True, stop=True)
                last.then_inc(sbu_full, 1)

            def s_scores(b):
                n = k_turn(b)
                keys = kcS[n % 3]
                pe.wait_ge(in_cache[n % 3], 16 * (n // 3 + 1))
                if b >= 1:
                    pe.wait_ge(ss_biased, b)
                for n0 in range(0, NK, 512):
                    n1 = min(n0 + 512, NK)
                    for c in range(CT):
                        last = mm(bankf[0:ST, n0:n1], qblk[:, b, c, :], keys[:, c, n0:n1],
                                  start=(c == 0), stop=(c == CT - 1))
                    if n1 == FIRST_BANKS:
                        last.then_inc(ss_first, 1)
                for c in range(CT):
                    last = mm(bankf[0:ST, NK:SK], qblk[:, b, c, :], kT[:, c, SEQ:TOK],
                              start=(c == 0), stop=(c == CT - 1))
                last.then_inc(ss_full, 1)

            def s_turn(b):
                pe.wait_ge(sp_ready, b + 1)
                if b >= 1:
                    pe.wait_ge(spt_ready, b)
                for k in range(KT + 1):
                    m = P if k < KT else ST
                    last = nc.tensor.transpose(bankf[0:m, 3 * 512 + k * ST:3 * 512 + (k + 1) * ST],
                                               pbuf[0:ST, b % 2, k * P:k * P + m], ident[0:ST, 0:ST])
                last.then_inc(sp_turned, 1)

            def s_values(b):
                n = v_turn(b)
                rows = vcS[n % 3]
                pe.wait_ge(spt_ready, b + 1)
                pe.wait_ge(in_cache[n % 3], 16 * (n // 3 + 1))
                if b >= 1:
                    pe.wait_ge(so_used, b)
                for c in range(CT):
                    o = bank[32 * c:32 * c + 16, 5, 0:P]
                    for k in range(KT + 1):
                        pt = ptS[:, b % 2, k * ST + 16 * c:k * ST + 16 * c + 16]
                        if k < KT:
                            mm(o, pt, rows[:, k, c * P:c * P + P], start=(k == 0), stop=False, skip_group_check=True)
                        else:
                            last = mm(o, pt[0:ST], vS[0:ST, QB, c * P:c * P + P], start=False, stop=True,
                                      skip_group_check=True)
                last.then_inc(so_full, 1)

            def s_turn_out(b):
                pe.wait_ge(so_copied, b + 1)
                nc.tensor.transpose(bank[:, 5, P:2 * P], oS, ident[:, :]).then_inc(so_turned, 1)

            def s_ssm_out():
                pe.wait_ge(sx_ready, 1)
                pe.wait_ge(sbu_used, 2)
                for j in range(SJ):
                    p0 = 32 * (j % 4)
                    for x in range(2):
                        last = mm(bank[p0:p0 + 32, 6, (j // 4) * ST:(j // 4 + 1) * ST], Craw[:, j, x, :],
                                  xs[x][:, j, :], start=(x == 0), stop=(x == 1), skip_group_check=True)
                last.then_inc(sy_full, 1)

            def glu_tile(c):
                if c == 0:
                    pe.wait_ge(in_glu, 16)
                    pe.wait_ge(z_ready, 1)
                else:
                    pe.wait_ge(sig_ready, c)
                for x in range(2):
                    for k in range(CT):
                        last = mm(bank[:, 6 + x, 0:WIDE], glu[:, k, c * P:c * P + P],
                                  zT[:, k, x * WIDE:(x + 1) * WIDE], start=(k == 0), stop=(k == CT - 1))
                last.then_inc(glu_full, 1)

            pe.wait_ge(qblk_set, 1)
            pe.wait_ge(sc_biased, len(UNITS))
            pe.wait_ge(pt_ready, len(UNITS))
            s_scores(0)
            s_ssm_in(0)
            s_ssm_in(1)
            for b in range(NB):
                s_turn(b)
                if b >= 1:
                    s_turn_out(b - 1)
                if b + 1 < NB:
                    s_scores(b + 1)
                if b == SSM_OUT_AT:
                    s_ssm_out()
                if b in GLU_BEFORE:
                    glu_tile(GLU_BEFORE[b])
                s_values(b)
                if b in GLU_AFTER:
                    glu_tile(GLU_AFTER[b])
            s_turn_out(NB - 1)

            pe.wait_ge(mixed, CT)
            pe.wait_ge(ones_set, 1)
            for b in range(BLOCKS):
                t0, m = tokens_of(b)
                for c in range(CT):
                    mm(bank[0:m, 7, b:b + 1], sq[:, c, t0:t0 + m], ones[:, 0:1], start=(c == 0), stop=(c == CT - 1))

            def project(b):
                t0, m = tokens_of(b)
                for half in range(2):
                    if b == 0:
                        pe.wait_ge(in_out[half], 16)
                    for part in range(2):
                        for k in range(CT):
                            last = mm(bank[0:m, OUT_BANK[b] + 2 * part + half, :],
                                      mixT[:, CT * part + k, t0:t0 + m], wout[half][:, CT * part + k, :],
                                      start=(k == 0), stop=(k == CT - 1))
                last.then_inc(out_full, 1)

            def turn_h(b, n):
                _, m = tokens_of(b)
                pe.wait_ge(h_ready, b + 1)
                if n >= 1:
                    pe.wait_ge(ht_ready, n)
                if 1 <= n <= BLOCKS:
                    pe.wait_ge(pq_ready, 4 * n)
                    pe.wait_ge(s_ready, 4 * n)
                for c in range(DC):
                    last = nc.tensor.transpose(bank[:, c // 4, (c % 4) * P:(c % 4) * P + m],
                                               hS[0:m, b, c * P:c * P + P], ident[0:m, 0:m])
                last.then_inc(ht_full, 1)

            def gate_turn(b):
                if b == 0:
                    pe.wait_ge(in_gate, 16 * 4)
                else:
                    pe.wait_ge(gate_used, 2 * b)
                turn_h(b, BLOCKS + b)

            def gate(b, half):
                t0, m = tokens_of(b)
                pe.wait_ge(ht_ready, BLOCKS + b + 1)
                to = 2 - 2 * half
                for k in range(2):
                    mm(bank[0:m, to + 1, :], pT[:, k, t0:t0 + m], ple[:, k, half * 512:half * 512 + 512],
                       start=(k == 0), stop=(k == 1))
                w = W[:, half, :].rearrange("p (c n) -> p c n", c=DC)
                for k in range(DC):
                    last = mm(bank[0:m, to, :], hT[:, k, 0:m], w[:, k, :], start=(k == 0), stop=(k == DC - 1))
                last.then_inc(gate_full, 1)

            def turn(b):
                turn_h(b, b)

            def ask(b, c):
                _, m = tokens_of(b)
                n = 4 * b + c
                if c == 0:
                    pe.wait_ge(ht_ready, b + 1)
                if b == 0:
                    pe.wait_ge(in_pq[c], 16)
                if n >= 2:
                    pe.wait_ge(pq_ready, n - 1)
                w = W[:, (c + 3) % 4, :].rearrange("p (c n) -> p c n", c=DC)
                for j in range(4):
                    for k in range(DC):
                        last = mm(bank[:, (2, 0)[c % 2], j * P:j * P + m], w[:, k, j * P:j * P + P],
                                  hT[:, k, 0:m], start=(k == 0), stop=(k == DC - 1))
                last.then_inc(pq_full, 1)

            def match(b, c):
                _, m = tokens_of(b)
                n = 4 * b + c
                pe.wait_ge(pq_ready, n + 1)
                if n >= 2:
                    pe.wait_ge(s_ready, n - 1)
                for j in range(4):
                    last = mm(bank[0:m, (3, 1)[c % 2], j * P:j * P + P], qpT[:, c % 2, j * P:j * P + m],
                              keysT[:, j % 2, :], start=True, stop=True)
                last.then_inc(s_full, 1)

            def experts(h0, h1):
                b = block_of(h0)
                _, m = tokens_of(b)
                acc = bankf[0:m, (4 + 2 * (b % 2)) * 512:(6 + 2 * (b % 2)) * 512]
                if h0 * HALF == b * EXP:
                    if b >= 2:
                        pe.wait_ge(acc_used, b - 1)
                    for half in range(2):
                        mm(acc[:, half * 512:half * 512 + 512], alpha_id[0:m, 0:m],
                           hS[0:m, b, half * 512:half * 512 + 512], start=True, stop=False, skip_group_check=True)

                def half_turn(i, x):
                    for r in range(HALF * x, HALF * x + HALF):
                        pe.wait_ge(diagonal, i * RING + (r + 1))
                        for half in range(2):
                            last = mm(acc[:, half * 512:half * 512 + 512], diag[:, r, 0:m],
                                      ring[r][:, D + half * 512:D + half * 512 + 512],
                                      start=False, stop=True, skip_group_check=True)
                        last.then_inc(slot_free, 1)

                turns(pe, h0, h1, half_turn)

            pe.wait_ge(at_done, QB)
            project(0)
            pe.wait_ge(so_used, NB)
            pe.wait_ge(asc_ready, 1)
            for c in range(CT):
                last = mm(bank[0:ST, 7, 8:9], asc[:, c, :], ones[:, 0:1], start=(c == 0), stop=(c == CT - 1))
            last.then_inc(sq_full, 1)
            pe.wait_ge(ssq_ready, 1)
            project(1)
            pe.wait_ge(in_keys, 16)
            pe.wait_ge(out_used, 1)
            turn(0)
            ask(0, 0)
            match(0, 0)
            pe.wait_ge(out_used, 2)
            project(2)
            pe.wait_ge(ht_ready, 1)
            pe.wait_ge(pq_ready, 1)
            pe.wait_ge(s_ready, 1)
            project(3)
            pe.wait_ge(out_used, 3)
            pe.wait_ge(mixed, CT + 1)
            project(4)
            pe.sem_inc(slot_free, RING - 2)
            pe.wait_ge(out_used, 4)
            ask(0, 1)
            match(0, 1)
            pe.wait_ge(alpha_set, 1)
            pe.wait_ge(out_used, BLOCKS)
            pe.wait_ge(h_ready, BLOCKS)
            pe.sem_inc(slot_free, 2)
            parts = {"turn": turn, "ask": ask, "match": match, "experts": experts, "gate_turn": gate_turn,
                     "gate": gate}
            for what, *at in ORDER:
                if what in parts:
                    parts[what](*at)

        @block.scalar
        def _(act):
            f = nc.scalar.activation
            n_link = [0]

            def link(ins):
                n_link[0] += 1
                ins.then_inc(act_chain, 1)
                act.wait_ge(act_chain, n_link[0])

            act.wait_ge(in_lam, 16)
            f(sm[:, 2, :], lam[:, 2, :], ACT.Exp).then_inc(exp_done, 1)
            act.wait_ge(ssm_exp_in, 1)
            f(sm[:, 3, :], sm[:, 4, :], ACT.Exp).then_inc(exp_done, 1)
            act.wait_ge(trig_arg, 1)
            f(sm[:, 7:9, :], sm[:, 5:7, :], ACT.Sin).then_inc(trig_done, 1)

            act.wait_ge(in_cols, 16)
            for n, (kind, c) in enumerate(PROJ):
                if kind in "ku":
                    act.wait_ge(proj_full, n + 1)
                    dst, col = (kT, 4 + c) if kind == "k" else (uT, 8 + c)
                    f(dst[:, c, :].rearrange("p (x t) -> p x t", x=2), bank[:, 2 * (n % 2):2 * (n % 2) + 2, 0:WIDE],
                      ACT.Identity, bias=cols[:, col:col + 1]).then_inc(k_done if kind == "k" else u_done, 1)

            act.wait_ge(q_done, CT)
            act.wait_ge(qblk_zero, 1)
            for c in range(CT):
                for e in range(2):
                    last = nc.scalar.copy(
                        qblk[64 * e:64 * e + 64, :, c, (2 * c + e) * NT:(2 * c + e + 1) * NT],
                        qT[64 * e:64 * e + 64, c, SEQ:TOK].rearrange("p (b t) -> p b t", t=NT))
            last.then_inc(qblk_set, 1)

            def exps(i):
                qb, _ = UNITS[i]
                n = P * (qb + 1)
                act.wait_ge(sc_biased, i + 1)
                f(pbuf[:, i % 2, 0:n], pbuf[:, i % 2, 0:n], ACT.Exp, bias=small[:, i % 2:i % 2 + 1],
                  accum_out=small[:, 4 + i % 4:5 + i % 4]).then_inc(p_ready, 1)

            def copy_pt(i):
                qb, _ = UNITS[i]
                n = P * (qb + 1)
                act.wait_ge(p_turned, i + 1)
                if i >= 2:
                    act.wait_ge(o_full, i - 1)
                nc.scalar.copy(ptS[:, i % 2, 0:n], bank[:, 2 + i % 2, 0:n]).then_inc(pt_ready, 1)

            def norm_out(i):
                qb, h = UNITS[i]
                act.wait_ge(o_full, i + 1)
                act.wait_ge(inverted, i + 1)
                if h == 0 and qb >= 2:
                    act.wait_ge(at_done, qb - 1)
                f(atok[:, qb % 2, h * HD:h * HD + HD], bank[:, 4, 0:HD], ACT.Copy,
                  scale=small[:, 12 + i % 4:13 + i % 4]).then_inc(o_normed, 1)

            def att_out(qb):
                act.wait_ge(o_normed, NH * (qb + 1))
                link(f(asc.rearrange("p a b -> p (a b)"), atok[:, qb % 2, 0:CT * ST], ACT.Square,
                       accum_out=small[:, 8 + 2 * (qb % 2):9 + 2 * (qb % 2)]))
                f(asc.rearrange("p a b -> p (a b)"), atok[:, qb % 2, CT * ST:AW], ACT.Square,
                  accum_out=small[:, 9 + 2 * (qb % 2):10 + 2 * (qb % 2)])
                act.wait_ge(at_full, qb + 1)
                for c in range(CT):
                    last = f(mixT[:, c, qb * P:qb * P + P], bank[:, 5, c * P:c * P + P], ACT.Copy,
                             scale=cols[:, 16 + c:17 + c])
                last.then_inc(at_done, 1)

            for i in range(len(UNITS) + 3):
                if i < len(UNITS):
                    exps(i)
                if 2 <= i < len(UNITS) + 2:
                    norm_out(i - 2)
                if 1 <= i <= len(UNITS):
                    copy_pt(i - 1)
                if i > 2 and (i - 2) % NH == 0:
                    att_out((i - 2) // NH - 1)

            act.wait_ge(o_full, len(UNITS))
            def copy_ssm_in(x):
                act.wait_ge(sbu_full, x + 1)
                nc.scalar.copy(xs[x].rearrange("p a b -> p (a b)"), bankf[:, 6 * 512:8 * 512]).then_inc(sbu_used, 1)

            def s_exp(b):
                act.wait_ge(ss_biased, b + 1)
                f(pbuf[0:ST, b % 2, :], pbuf[0:ST, b % 2, :], ACT.Exp, bias=small[0:ST, b % 2:b % 2 + 1],
                  accum_out=small[0:ST, 4 + b % 2:5 + b % 2]).then_inc(sp_exp, 1)

            def s_copy(b):
                act.wait_ge(sp_turned, b + 1)
                if b >= 2:
                    act.wait_ge(so_full, b - 1)
                nc.scalar.copy(ptS[:, b % 2, 0:KT * ST], bankf[:, 3 * 512:3 * 512 + KT * ST])
                nc.scalar.copy(ptS[0:ST, b % 2, KT * ST:(KT + 1) * ST],
                               bankf[0:ST, 3 * 512 + KT * ST:3 * 512 + (KT + 1) * ST]).then_inc(spt_ready, 1)

            def s_copy_out(b):
                act.wait_ge(so_full, b + 1)
                if b == 0:
                    act.wait_ge(os_zero, 1)
                else:
                    act.wait_ge(so_turned, b)
                for c in range(CT):
                    last = nc.scalar.copy(oS[32 * c:32 * c + 16], bank[32 * c:32 * c + 16, 5, 0:P])
                last.then_inc(so_copied, 1)

            def z_gelu():
                act.wait_ge(sy_used, 1)
                z = zT.rearrange("p a b -> p (a b)")
                f(z, z, ACT.Gelu_apprx_tanh).then_inc(z_ready, 1)

            def glu_gate(c):
                act.wait_ge(glu_full, c + 1)
                if c >= 2:
                    act.wait_ge(mixed, c - 1)
                f(sg[c % 2].rearrange("p (x t) -> p x t", x=2), bank[:, 6:8, 0:WIDE], ACT.Sigmoid,
                  bias=cols[:, 12 + c:13 + c]).then_inc(sig_ready, 1)

            act.wait_ge(carried, 4 * QB)
            copy_ssm_in(0)
            s_exp(0)
            copy_ssm_in(1)
            for b in range(NB):
                if b >= 1:
                    s_copy_out(b - 1)
                s_copy(b)
                if b - 1 in GLU_AFTER:
                    glu_gate(GLU_AFTER[b - 1])
                if b + 1 < NB:
                    s_exp(b + 1)
                if b == SSM_OUT_AT:
                    z_gelu()
                if b in GLU_BEFORE:
                    glu_gate(GLU_BEFORE[b])
            s_copy_out(NB - 1)

            def copy_ht(b, n):
                _, m = tokens_of(b)
                act.wait_ge(ht_full, n + 1)
                if 1 <= n <= BLOCKS:
                    act.wait_ge(pq_full, 4 * n)
                elif n > BLOCKS:
                    act.wait_ge(gate_full, 2 * (n - BLOCKS))
                src = bank[:, 0:2, :].rearrange("p a (b t) -> p (a b) t", b=4)
                nc.scalar.copy(hT[:, :, 0:m], src[:, :, 0:m]).then_inc(ht_ready, 1)

            def gate_turn(b):
                copy_ht(b, BLOCKS + b)

            def gate_out(b, half):
                _, m = tokens_of(b)
                act.wait_ge(gate_full, 2 * b + half + 1)
                if 2 * b + half >= 1:
                    act.wait_ge(gate_used, 2 * b + half)
                f(sgm[0:m], bank[0:m, 2 - 2 * half, :], ACT.Sigmoid).then_inc(gate_sig, 1)

            def turn(b):
                copy_ht(b, b)

            def ask_out(b, c):
                _, m = tokens_of(b)
                n = 4 * b + c
                act.wait_ge(pq_full, n + 1)
                if n >= 2:
                    act.wait_ge(s_full, n - 1)
                src = bank[:, (2, 0)[c % 2], :].rearrange("p (a t) -> p a t", t=P)
                dst = qpT[:, c % 2, :].rearrange("p (a t) -> p a t", t=P)
                nc.scalar.copy(dst[:, :, 0:m], src[:, :, 0:m]).then_inc(pq_ready, 1)

            def match_out(b, c):
                _, m = tokens_of(b)
                n = 4 * b + c
                act.wait_ge(s_full, n + 1)
                if n >= 2:
                    act.wait_ge(s_used, n - 1)
                nc.scalar.copy(sS[0:m, c % 2, :, :].rearrange("p a b -> p (a b)"),
                               bank[0:m, (3, 1)[c % 2], :]).then_inc(s_ready, 1)

            def cross(b, c):
                _, m = tokens_of(b)
                act.wait_ge(gx_ready, 4 * b + c + 1)
                f(gx[0:m], gx[0:m], ACT.Exp).then_inc(gexp_done, 1)

            def copy_stage(half, at):
                return nc.scalar.copy(stage[:, half, :], eall[:, at])

            def experts(h0, h1):
                b = block_of(h0)
                _, m = tokens_of(b)
                sel = ident if b < QB else fold
                if (h1 + 1) * HALF < QB * EXP:
                    act.wait_ge(picked, (h1 + 1) * HALF // (2 * PK) + 1)
                else:
                    act.wait_ge(picked, 4 * BLOCKS)
                    act.wait_ge(packed, 32)
                def half_turn(i, x):
                    for g in range(HALF // PAIR):
                        n = 4 * i + (2 * x + g + 1)
                        act.wait_ge(dotted, n)
                        if g == 1:
                            copy_stage(x, column(i, RING + x * HALF, HALF)).then_inc(staged, 1)
                        two = slice(g * PAIR, g * PAIR + PAIR)
                        f(gel[:, x, two], dots[:, x, two], ACT.Gelu_apprx_tanh).then_inc(gelued, 1)
                        act.wait_ge(gelued, n)
                        for s in range(g * PAIR, g * PAIR + PAIR):
                            last = f(wts[:, x, s:s + 1], gel[:, x, s:s + 1], ACT.Copy,
                                     scale=gall[:, column(i, x * HALF + s, 1)])
                        last.then_inc(weighed, 1)
                        act.wait_ge(weighed, n)
                        for s in range(g * PAIR, g * PAIR + PAIR):
                            f(diag[:, x * HALF + s, 0:m], sel[:, 0:m], ACT.Copy,
                              scale=wts[:, x, s:s + 1]).then_inc(diagonal, 1)

                turns(act, h0, h1, half_turn)

            def ln_roots(b):
                act.wait_ge(var_ready, b + 1)
                f(rstd[:, b:b + 1], rstd[:, b:b + 1], ACT.Sqrt).then_inc(ln_root, 1)

            act.wait_ge(ssq_ready, 1)
            f(ssq[:, :, :], ssq[:, :, :], ACT.Sqrt).then_inc(rms_root, 1)
            ln_roots(0)
            turn(0)
            ln_roots(1)
            ask_out(0, 0)
            match_out(0, 0)
            cross(0, 0)
            act.wait_ge(picked, 1)
            for half in range(2):
                copy_stage(half, slice(half * HALF, half * HALF + HALF)).then_inc(staged, 1)
            for b in range(2, BLOCKS):
                ln_roots(b)
            ask_out(0, 1)
            match_out(0, 1)

            def finish(b):
                act.wait_ge(y_var, b + 1)
                f(lnrow[:, 2:3], lnrow[:, 1:2], ACT.Sqrt).then_inc(y_root, 1)

            parts = {"turn": turn, "ask_out": ask_out, "match_out": match_out, "cross": cross,
                     "experts": experts, "gate_turn": gate_turn, "gate_out": gate_out, "finish": finish}
            for what, *at in ORDER:
                if what in parts:
                    parts[what](*at)

        @block.vector
        def _(dve):
            tt = nc.vector.tensor_tensor
            tsc = nc.vector.tensor_scalar
            stt = nc.vector.scalar_tensor_tensor
            n_link = [0]

            def link(ins):
                n_link[0] += 1
                ins.then_inc(dve_chain, 1)
                dve.wait_ge(dve_chain, n_link[0])

            def mark(ins):
                n_link[0] += 1
                ins.then_inc(dve_chain, 1)
                return n_link[0]

            def after(n):
                dve.wait_ge(dve_chain, n)

            dve.wait_ge(in_lam, 16)
            dve.wait_ge(exp_done, 1)
            tt(sm[:, 4, :], lam[:, 0, :], sm[:, 2, :], ALU.mult).then_inc(ssm_exp_in, 1)
            link(tt(sm[:, 5, :], lam[:, 1, :], sm[:, 2, :], ALU.mult))
            link(tsc(sm[:, 6, :], sm[:, 5, :], float(np.pi / 2), None, ALU.add))
            th, kk = sm[:, 5:7, :], sm[:, 18:20, :]
            link(tsc(kk, th, float(1 / TWO_PI), ROUND, ALU.mult, ALU.add))
            link(tsc(kk, kk, ROUND, None, ALU.subtract))
            link(stt(th, kk, -TP_HI, th, ALU.mult, ALU.add))
            link(stt(th, kk, -float(TP_LO), th, ALU.mult, ALU.add))
            tsc(th, th, -3.1415925, 3.1415925, ALU.max, ALU.min).then_inc(trig_arg, 1)
            dve.wait_ge(trig_done, 1)
            dve.wait_ge(exp_done, 2)
            tt(sm[:, 0, :], sm[:, 3, :], sm[:, 8, :], ALU.mult)
            link(tt(sm[:, 1, :], sm[:, 3, :], sm[:, 7, :], ALU.mult))
            tt(sm[:, 18, :], lam[:, 0, :], lam[:, 0, :], ALU.mult)
            tt(sm[:, 19, :], lam[:, 1, :], lam[:, 1, :], ALU.mult)
            link(tsc(sm[:, 9, :], sm[:, 0, :], -1.0, None, ALU.add))
            link(tt(sm[:, 18, :], sm[:, 18, :], sm[:, 19, :], ALU.add))
            link(nc.vector.reciprocal(sm[:, 12, :], sm[:, 18, :]))
            tt(sm[:, 10, :], sm[:, 9, :], lam[:, 0, :], ALU.mult)
            tt(sm[:, 11, :], sm[:, 1, :], lam[:, 0, :], ALU.mult)
            tt(sm[:, 18, :], sm[:, 1, :], lam[:, 1, :], ALU.mult)
            link(tt(sm[:, 19, :], sm[:, 9, :], lam[:, 1, :], ALU.mult))
            tt(sm[:, 10, :], sm[:, 10, :], sm[:, 18, :], ALU.add)
            link(tt(sm[:, 11, :], sm[:, 11, :], sm[:, 19, :], ALU.subtract))
            tt(sm[:, 10, :], sm[:, 10, :], sm[:, 12, :], ALU.mult)
            link(tt(sm[:, 11, :], sm[:, 11, :], sm[:, 12, :], ALU.mult))

            def wide(k, n):
                return sm[:, k, :].unsqueeze(2).broadcast_to([P, SJ, n])

            def q_done_job(c):
                n = PROJ.index(("q", c))
                dve.wait_ge(proj_full, n + 1)
                tsc(qT[:, c, :].rearrange("p (x t) -> p x t", x=2), bank[:, 2 * (n % 2):2 * (n % 2) + 2, 0:WIDE],
                    cols[:, c:c + 1], HD ** -0.5, ALU.add, ALU.mult).then_inc(q_done, 1)

            dve.wait_ge(in_cols, 16)
            for c in range(CT):
                q_done_job(c)

            dve.wait_ge(in_ssm, 16 * 2)
            c4 = [w[:, 0:512].rearrange("p (a b) -> p a b", b=32) for w in wt]
            tt(c4[0], Craw[:, :, 0, :], wide(10, 32), ALU.mult)
            tt(c4[1], Craw[:, :, 1, :], wide(11, 32), ALU.mult)
            tt(c4[2], Craw[:, :, 0, :], wide(11, 32), ALU.mult)
            link(tt(c4[3], Craw[:, :, 1, :], wide(10, 32), ALU.mult))
            tt(Csc[:, :, 0, :], c4[0], c4[1], ALU.subtract)
            link(tt(c4[2], c4[2], c4[3], ALU.add))
            tsc(Csc[:, :, 1, :], c4[2], -1.0, None, ALU.mult)
            link(tsc(Craw[:, :, 1, :], Craw[:, :, 1, :], -1.0, None, ALU.mult))

            nc.vector.memset(tc[:, :, 0:1], 1.0)
            nc.vector.memset(ts[:, :, 0:1], 0.0)
            nc.vector.tensor_copy(sm[:, 12, :], sm[:, 8, :])
            nc.vector.tensor_copy(tm, wide(3, P))
            link(nc.vector.tensor_copy(sm[:, 13, :], sm[:, 7, :]))
            nc.vector.memset(tm[:, :, 0:1], 0.0)

            def v_done_job(b):
                _, m = tokens_of(b)
                n = PROJ.index(("v", b))
                dve.wait_ge(proj_full, n + 1)
                tt(vS[0:m, b, :], bank[0:m, 2 * (n % 2), :], vrow[0:m], ALU.add).then_inc(v_done, 1)

            dve.wait_ge(in_vrow, 16)
            n = 1
            while n < P:
                w = [x[:, 0:SJ * n].rearrange("p (a b) -> p a b", b=n) for x in wt]
                tt(w[0], tc[:, :, 0:n], wide(12, n), ALU.mult)
                tt(w[1], ts[:, :, 0:n], wide(13, n), ALU.mult)
                tt(w[2], tc[:, :, 0:n], wide(13, n), ALU.mult)
                link(tt(w[3], ts[:, :, 0:n], wide(12, n), ALU.mult))
                tt(tc[:, :, n:2 * n], w[0], w[1], ALU.subtract)
                tt(ts[:, :, n:2 * n], w[2], w[3], ALU.add)
                tt(sm[:, 18, :], sm[:, 12, :], sm[:, 12, :], ALU.mult)
                tt(sm[:, 19, :], sm[:, 13, :], sm[:, 13, :], ALU.mult)
                link(tt(sm[:, 9, :], sm[:, 12, :], sm[:, 13, :], ALU.mult))
                tt(sm[:, 12, :], sm[:, 18, :], sm[:, 19, :], ALU.subtract)
                link(tsc(sm[:, 13, :], sm[:, 9, :], 2.0, None, ALU.mult))
                n *= 2
            nc.vector.memset(small[:, :], 0.0)
            link(nc.vector.memset(ssq[:, :, :], 1.0))
            nc.vector.tensor_copy(sm[:, 9, :], sm[:, 0, :]).then_inc(tables_done, 1)
            for b in range(BLOCKS):
                v_done_job(b)

            def add_bias(i):
                qb, h = UNITS[i]
                m = P * (qb + 1)
                dve.wait_ge(sc_full, i + 1)
                if i >= 2:
                    dve.wait_ge(p_turned, i - 1)
                link(nc.vector.tensor_tensor_reduce(
                    pbuf[:, i % 2, 0:m], bank[:, i % 2, 0:m], pbias[:, h, SEQ - m:SEQ], 1.0, NEG,
                    ALU.add, ALU.max, small[:, 2 + i % 2:3 + i % 2]))
                tsc(small[:, i % 2:i % 2 + 1], small[:, 2 + i % 2:3 + i % 2], -1.0, None, ALU.mult).then_inc(sc_biased, 1)

            def invert(i):
                dve.wait_ge(p_ready, i + 1)
                nc.vector.reciprocal(small[:, 12 + i % 4:13 + i % 4], small[:, 4 + i % 4:5 + i % 4]).then_inc(
                    inverted, 1)

            def keep_squares(qb):
                dve.wait_ge(at_done, qb + 1)
                tt(ssq[:, 0, qb:qb + 1], small[:, 8 + 2 * (qb % 2):9 + 2 * (qb % 2)],
                   small[:, 9 + 2 * (qb % 2):10 + 2 * (qb % 2)], ALU.add)

            def flat(x):
                return x.rearrange("p a b -> p (a b)")

            def scan(n):
                b, q = divmod(n, 4)
                j = slice(4 * q, 4 * q + 4)
                c_, s_ = tc[:, j, :], ts[:, j, :]
                re = bank[:, 6, :].rearrange("p (a t) -> p a t", t=P)
                im = bank[:, 7, :].rearrange("p (a t) -> p a t", t=P)
                r_re, r_im, t1, t2, t3, t4 = rr
                p_rc, p_is, p_rs, p_ic = turned[n % 2]
                dve.wait_ge(bu_full, n + 1)
                tt(t1, re, c_, ALU.mult)
                m12 = mark(tt(t2, im, s_, ALU.mult))
                tt(t3, im, c_, ALU.mult)
                tt(t4, re, s_, ALU.mult).then_inc(bu_used, 1)
                after(m12)
                m_re = mark(tt(r_re, t1, t2, ALU.add))
                dve.wait_ge(bu_used, n + 1)
                m_im = mark(tt(r_im, t3, t4, ALU.subtract))
                if b > 0:
                    dve.wait_ge(carried, n - 3)
                    after(m_re)
                    m_re = mark(tt(r_re[:, :, 0], r_re[:, :, 0], sm[:, 16, j], ALU.add))
                    after(m_im)
                    m_im = mark(tt(r_im[:, :, 0], r_im[:, :, 0], sm[:, 17, j], ALU.add))
                m = flat(tm[:, j, :])
                after(m_re)
                m_re = mark(nc.vector.tensor_tensor_scan(flat(t1), m, flat(r_re), 0.0, ALU.mult, ALU.add))
                after(m_im)
                m_im = mark(nc.vector.tensor_tensor_scan(flat(t2), m, flat(r_im), 0.0, ALU.mult, ALU.add))
                if n >= 2:
                    dve.wait_ge(y_full, n - 1)
                    dve.wait_ge(carried, n - 1)
                after(m_re)
                tt(p_rc, t1, c_, ALU.mult)
                tt(p_rs, t1, s_, ALU.mult)
                after(m_im)
                tt(p_is, t2, s_, ALU.mult)
                tt(p_ic, t2, c_, ALU.mult).then_inc(hs_ready, 1)

            def skip_term(n):
                b, q = divmod(n, 4)
                dve.wait_ge(y_full, n + 1)
                stt(zT[:, q, b * P:b * P + P], uT[:, q, b * P:b * P + P], cols[:, 24 + q:25 + q],
                    bank[:, 5, 0:P], ALU.mult, ALU.add).then_inc(y_used, 1)

            dve.wait_ge(in_pb, 16)
            dve.wait_ge(u_done, CT)
            tsc(Cneg, Csc[:, :, 0, :], -1.0, None, ALU.mult).then_inc(cneg_set, 1)
            for i in range(len(UNITS) + 4):
                if i < len(UNITS):
                    add_bias(i)
                if 1 <= i <= len(UNITS):
                    invert(i - 1)
                if i % 2 == 1 and i // 2 >= 2:
                    skip_term(i // 2 - 2)
                if i % 2 == 1 and i // 2 < 4 * QB:
                    scan(i // 2)
                if 4 <= i <= len(UNITS) and (i - 3) % NH == 0:
                    keep_squares((i - 3) // NH - 1)
            keep_squares(QB - 1)
            nc.vector.tensor_copy(sm[:, 9, :], sm[:, 0, :]).then_inc(hs_ready, 1)

            def s_bias(b):
                dve.wait_ge(ss_first, b + 1)
                if b >= 2:
                    dve.wait_ge(sp_turned, b - 1)
                nc.vector.tensor_tensor_reduce(
                    pbuf[0:ST, b % 2, 0:FIRST_BANKS], bankf[0:ST, 0:FIRST_BANKS], sbias[0:ST, 0:FIRST_BANKS],
                    1.0, NEG, ALU.add, ALU.max, small[0:ST, 8:9])
                dve.wait_ge(ss_full, b + 1)
                nc.vector.tensor_tensor_reduce(
                    pbuf[0:ST, b % 2, FIRST_BANKS:NK], bankf[0:ST, FIRST_BANKS:NK], sbias[0:ST, FIRST_BANKS:NK],
                    1.0, NEG, ALU.add, ALU.max, small[0:ST, 10:11])
                link(nc.vector.tensor_tensor_reduce(
                    pbuf[0:ST, b % 2, NK:SK], bankf[0:ST, NK:SK], sbias[0:ST, NK + b * ST:NK + (b + 1) * ST], 1.0, NEG,
                    ALU.add, ALU.max, small[0:ST, 9:10]))
                link(nc.vector.tensor_reduce(small[0:ST, 8:9], small[0:ST, 8:11], AX.X, ALU.max))
                tsc(small[0:ST, b % 2:b % 2 + 1], small[0:ST, 8:9], -1.0, None, ALU.mult).then_inc(ss_biased, 1)

            def s_norm(b):
                dve.wait_ge(sp_exp, b + 1)
                link(nc.vector.reciprocal(small[0:ST, 12:13], small[0:ST, 4 + b % 2:5 + b % 2]))
                tsc(pbuf[0:ST, b % 2, :], pbuf[0:ST, b % 2, :], small[0:ST, 12:13], None, ALU.mult).then_inc(sp_ready, 1)

            def s_out(b):
                dve.wait_ge(so_turned, b + 1)
                for e in range(2):
                    src = bank[64 * e:64 * e + 64, 5, P:2 * P].rearrange("p (c g) -> p c g", c=CT)
                    last = nc.vector.tensor_copy(
                        mixT[64 * e:64 * e + 64, 0:CT, SEQ + b * NT:SEQ + (b + 1) * NT],
                        src[:, :, e * NT:(e + 1) * NT])
                last.then_inc(so_used, 1)

            def s_skip_term():
                dve.wait_ge(sy_full, 1)
                for q in range(CT):
                    last = stt(zT[:, q, SEQ:TOK], uT[:, q, SEQ:TOK], cols[:, 24 + q:25 + q],
                               bank[:, 6, q * ST:(q + 1) * ST], ALU.mult, ALU.add)
                last.then_inc(sy_used, 1)

            def glu_product(c):
                dve.wait_ge(sig_ready, c + 1)
                link(tt(sg[c % 2], sg[c % 2], zT[:, c, :], ALU.mult))
                tt(sq[:, c, :], sg[c % 2], sg[c % 2], ALU.mult)
                tsc(mixT[:, CT + c, :], sg[c % 2], cols[:, 20 + c:21 + c], None, ALU.mult).then_inc(mixed, 1)

            dve.wait_ge(in_sb, 16)
            dve.wait_ge(hs_ready, 4 * QB + 1)
            s_bias(0)
            s_norm(0)
            for b in range(NB):
                if b >= 1:
                    s_out(b - 1)
                if b - 1 in GLU_AFTER:
                    glu_product(GLU_AFTER[b - 1])
                if b + 1 < NB:
                    s_bias(b + 1)
                    s_norm(b + 1)
                if b == SSM_OUT_AT:
                    s_skip_term()
                if b in GLU_BEFORE:
                    glu_product(GLU_BEFORE[b])
            s_out(NB - 1)
            dve.wait_ge(so_used, NB)
            tt(asc, mixT[:, 0:CT, SEQ:TOK], mixT[:, 0:CT, SEQ:TOK], ALU.mult).then_inc(asc_ready, 1)
            dve.wait_ge(asc_ready, 1)
            for c in range(CT):
                last = tsc(mixT[:, c, SEQ:TOK], mixT[:, c, SEQ:TOK], cols[:, 16 + c:17 + c], None, ALU.mult)
            last.then_inc(mixed, 1)
            dve.wait_ge(sq_full, 1)
            nc.vector.tensor_copy(ssq[:, 1, 0:QB], bank[:, 7, 0:QB])
            nc.vector.tensor_copy(ssq[0:ST, 1, QB:BLOCKS], bank[0:ST, 7, QB:BLOCKS])
            link(nc.vector.tensor_copy(ssq[0:ST, 0, QB:BLOCKS], bank[0:ST, 7, 8:9]))
            tsc(ssq[:, :, :], ssq[:, :, :], 1.0 / AW, EPS, ALU.mult, ALU.add).then_inc(ssq_ready, 1)
            dve.wait_ge(rms_root, 1)
            link(nc.vector.reciprocal(ssq[:, :, :], ssq[:, :, :]))

            def best16(v, i, x, m):
                link(nc.vector.max(v[:, 0:8], x))
                nc.vector.max_index(i[:, 0:8], v[:, 0:8], x)
                link(nc.vector.match_replace(sw[0:m, 0:x.shape[1]], v[:, 0:8], x, NEG))
                link(nc.vector.max(v[:, 8:16], sw[0:m, 0:x.shape[1]]))
                return nc.vector.max_index(i[:, 8:16], v[:, 8:16], sw[0:m, 0:x.shape[1]])

            def tops(b, c, half):
                _, m = tokens_of(b)
                n = 4 * b + c
                if half == 0:
                    dve.wait_ge(s_ready, n + 1)
                for j in range(2 * half, 2 * half + 2):
                    last = best16(tv[0:m, j, :], ti[0:m, j, :], sS[0:m, c % 2, j, :], m)
                    if j < 3:
                        link(last)
                if half == 1:
                    last.then_inc(s_used, 1)

            def cross(b, c):
                _, m = tokens_of(b)
                n = 4 * b + c
                dve.wait_ge(s_used, n + 1)
                for e in range(2):
                    a = tv[0:m, 2 * e, :].unsqueeze(2).broadcast_to([m, PK, PK])
                    d = tv[0:m, 2 * e + 1, :].unsqueeze(1).broadcast_to([m, PK, PK])
                    link(tt(cand[0:m, e, :].rearrange("p (a b) -> p a b", b=PK), a, d, ALU.add))
                    link(best16(sc[0:m, e, :], ci[0:m, e, :], cand[0:m, e, :], m))
                tt(gx[0:m], sc[0:m], sc[0:m, :, 0:1].broadcast_to([m, 2, PK]), ALU.subtract).then_inc(gx_ready, 1)

            def resolve(b, c):
                _, m = tokens_of(b)
                n = 4 * b + c
                cif = ci[0:m].rearrange("p a b -> p (a b)")
                tsc(cab[0:m, 0, :], cif, 4, None, ALU.logical_shift_right)
                nc.vector.tensor_copy(tif[0:m], ti[0:m])
                link(tsc(cab[0:m, 1, :], cif, 15, None, ALU.bitwise_and))
                link(nc.vector.tensor_copy(cabf[0:m], cab[0:m]))
                for x in range(2):
                    sel = cabf[0:m, x, :].unsqueeze(2).broadcast_to([m, 2 * PK, PK])
                    link(tt(oh[0:m], sel, iota[0:m, :].unsqueeze(1).broadcast_to([m, 2 * PK, PK]), ALU.is_equal))
                    key = tif[0:m].rearrange("p (h x) a -> p h x a", x=2)[:, :, x, :]
                    o4 = oh[0:m].rearrange("p (h k) a -> p h k a", k=PK)
                    link(tt(o4, o4, key.unsqueeze(2).broadcast_to([m, 2, PK, PK]), ALU.mult))
                    link(nc.vector.tensor_reduce(e12[0:m, x, :], oh[0:m], AX.X, ALU.add))
                link(stt(efl[0:m], e12[0:m, 0, :], float(NKEY), e12[0:m, 1, :], ALU.mult, ALU.add))
                dve.wait_ge(gexp_done, n + 1)
                link(nc.vector.tensor_reduce(gsm[0:m], gx[0:m], AX.X, ALU.add))
                link(nc.vector.reciprocal(gsm[0:m], gsm[0:m]))
                if b < QB or c < 2:
                    at = b * EXP + 2 * PK * c
                    e_to, g_to = eall[0:m, at:at + 2 * PK], gall[0:m, at:at + 2 * PK]
                else:
                    at = 2 * PK * (c - 2)
                    e_to, g_to = up_e[0:m, at:at + 2 * PK], up_g[0:m, at:at + 2 * PK]
                if n == 4 * BLOCKS - 1:
                    nc.vector.memset(eall[:, STEPS:STEPS + RING].bitcast(F32), 0.0)
                nc.vector.tensor_copy(e_to, efl[0:m])
                tt(g_to.rearrange("p (a b) -> p a b", b=PK), gx[0:m],
                   gsm[0:m].unsqueeze(2).broadcast_to([m, 2, PK]), ALU.mult).then_inc(picked, 1)

            def residual(b):
                _, m = tokens_of(b)
                link(stt(hS[0:m, b, :], hS[0:m, b, :], ALPHA, rows1[0:m, 0, :], ALU.mult, ALU.add))
                dve.wait_ge(out_full, b + 1)
                o = OUT_BANK[b] * 512
                link(stt(hS[0:m, b, :], bankf[0:m, o:o + D], ssq[0:m, 0, b:b + 1], hS[0:m, b, :], ALU.mult, ALU.add))
                stt(hS[0:m, b, :], bankf[0:m, o + D:o + 2 * D], ssq[0:m, 1, b:b + 1], hS[0:m, b, :],
                    ALU.mult, ALU.add).then_inc(out_used, 1)
                dve.wait_ge(out_used, b + 1)
                for x in range(2):
                    last = nc.vector.bn_stats(stats[0:m, 6 * x:6 * x + 6], hS[0:m, b, x * 512:x * 512 + 512])
                link(last)
                link(nc.vector.bn_aggr(mv[0:m, b, :], stats[0:m, :]))
                tsc(rstd[:, b:b + 1], mv[:, b, 1:2], EPS, None, ALU.add).then_inc(var_ready, 1)

            def normal(b):
                _, m = tokens_of(b)
                dve.wait_ge(ln_root, b + 1)
                link(nc.vector.reciprocal(rstd[0:m, b:b + 1], rstd[0:m, b:b + 1]))
                link(tsc(hS[0:m, b, :], hS[0:m, b, :], mv[0:m, b, 0:1], rstd[0:m, b:b + 1], ALU.subtract, ALU.mult))
                link(tt(hS[0:m, b, :], hS[0:m, b, :], rows1[0:m, 1, :], ALU.mult))
                tt(hS[0:m, b, :], hS[0:m, b, :], rows1[0:m, 2, :], ALU.add).then_inc(h_ready, 1)

            link(nc.vector.memset(mv[:, :, :], 1.0))
            dve.wait_ge(in_rows1, 16)
            dve.wait_ge(in_xr, 16 * BLOCKS)
            for b in range(BLOCKS):
                residual(b)
                normal(b)
                if b == 1:
                    tops(0, 0, 0)
                    tops(0, 0, 1)
                    cross(0, 0)
                    resolve(0, 0)
            tsc(alpha_id, ident[:, :], ALPHA, None, ALU.mult).then_inc(alpha_set, 1)

            def experts(h0, h1):
                b = block_of(h0)
                if h0 * HALF == QB * EXP:
                    dve.wait_ge(hdup, 16)

                def half_turn(i, x):
                    for s in range(HALF):
                        r = x * HALF + s
                        dve.wait_ge(landed[r], 16 * i + 16)
                        last = nc.vector.tensor_tensor_reduce(
                            ring[r][:, 0:D], ring[r][:, 0:D], hS[:, b, :], 1.0, 0.0, ALU.mult, ALU.add,
                            dots[:, x, s:s + 1])
                        if s % PAIR == PAIR - 1:
                            last.then_inc(dotted, 1)

                turns(dve, h0, h1, half_turn)

            def gate_out(b, half):
                _, m = tokens_of(b)
                dve.wait_ge(gate_sig, 2 * b + half + 1)
                tt(gp[0:m, b % 4, half * 512:half * 512 + 512], sgm[0:m], bank[0:m, 3 - 2 * half, :],
                   ALU.mult).then_inc(gate_used, 1)

            def sum_of(b):
                _, m = tokens_of(b)
                dve.wait_ge(slot_free, RING + (EXP * (b + 1) if b < QB else STEPS))
                return bankf[0:m, (4 + 2 * (b % 2)) * 512:(6 + 2 * (b % 2)) * 512]

            def put_by(b):
                nc.vector.tensor_copy(keep, sum_of(b)).then_inc(acc_used, 1)
                dve.wait_ge(acc_used, b + 1)

            def finish(b):
                _, m = tokens_of(b)
                dve.wait_ge(gate_used, 2 * b + 2)
                if b >= 1:
                    dve.wait_ge(ysem, 16 * b)
                if b == 0:
                    link(tt(ybuf[0:m], keep[0:m], gp[0:m, b % 4, :], ALU.add))
                else:
                    tt(ybuf[0:m], sum_of(b), gp[0:m, b % 4, :], ALU.add).then_inc(acc_used, 1)
                    dve.wait_ge(acc_used, b + 1)
                for x in range(2):
                    last = nc.vector.bn_stats(stats[0:m, 6 * x:6 * x + 6], ybuf[0:m, x * 512:x * 512 + 512])
                link(last)
                link(nc.vector.bn_aggr(lnrow[0:m, 0:2], stats[0:m, :]))
                tsc(lnrow[:, 1:2], lnrow[:, 1:2], EPS, None, ALU.add).then_inc(y_var, 1)
                dve.wait_ge(y_root, b + 1)
                link(nc.vector.reciprocal(lnrow[:, 3:4], lnrow[:, 2:3]))
                link(tsc(ybuf[0:m], ybuf[0:m], lnrow[0:m, 0:1], lnrow[0:m, 3:4], ALU.subtract, ALU.mult))
                link(tt(ybuf[0:m], ybuf[0:m], rows2[0:m, 0, :], ALU.mult))
                tt(ybuf[0:m], ybuf[0:m], rows2[0:m, 1, :], ALU.add).then_inc(y_made, 1)

            dve.wait_ge(in_rows2, 16)
            parts = {"tops": tops, "cross": cross, "resolve": resolve, "experts": experts, "gate_out": gate_out,
                     "put_by": put_by, "finish": finish}
            for what, *at in ORDER:
                if what in parts:
                    parts[what](*at)


def multiplicity(d):
    return sum(((d >= 0) & (d <= w) & (d % s == 0)).astype(np.float64) for w, s in BRANCHES)


def bias_of(d, slope):
    m = multiplicity(d)
    return np.where(m > 0, -slope * d + np.log(np.maximum(m, 1)), -1.0e30).astype(np.float32)


def tiles(w, parts):
    k, n = w.shape
    return np.ascontiguousarray(w.reshape(k // P, P, parts, n // parts).transpose(2, 1, 0, 3).reshape(parts, P, -1))


def by_channel(v):
    return v.reshape(-1, P).T


def spread(v):
    return np.broadcast_to(v, (P,) + v.shape)


def cache_order():
    r = np.arange(PAST)
    old = r < PAST - 512
    return np.concatenate([r[old & (r % 16 < NT)], r[~old], r[old & (r % 16 >= NT)]])


def layouts(i):
    sq = {k: np.asarray(v) for k, v in i.items()}
    x = np.concatenate([sq["x_prompt"].reshape(SEQ, D), sq["x_sample"].reshape(ST, D)])
    p = np.concatenate([sq["p_prompt"].reshape(SEQ, PLE), sq["p_sample"].reshape(ST, PLE)])
    order = cache_order()
    b_in = sq["b_in"][0]
    a = {"x_rows": x, "xT": x.T.reshape(DC, P, TOK).transpose(1, 0, 2),
         "pT": p.T.reshape(2, P, TOK).transpose(1, 0, 2)}
    a["w_in"] = tiles(sq["w_in"][0], 4)
    a["w_out"] = tiles(sq["w_out"][0], 2)
    a["w_gate"] = tiles(sq["w_ple_gate"][0], 2)
    a["w_pq"] = tiles(sq["w_pq"][0], 4)
    a["glu"] = tiles(sq["w_glu"][0], 1)[0].reshape(P, CT, AW)
    a["w_ple"] = tiles(sq["w_ple"][0], 1)[0].reshape(P, 2, D)
    a["vrow"] = spread(b_in[2 * AW:3 * AW])
    a["cols"] = np.concatenate(
        [by_channel(b_in[0:AW]), by_channel(b_in[AW:2 * AW]), by_channel(b_in[3 * AW:])]
        + [by_channel(sq[n][0].reshape(-1)) for n in ("b_glu", "g_att_out", "g_ssm_out", "ssm_d")], axis=1)
    a["rows1"] = spread(np.stack([sq["b_out"][0], sq["ln1_g"][0], sq["ln1_b"][0]]))
    a["rows2"] = spread(np.stack([sq["ln2_g"][0], sq["ln2_b"][0]]))

    def states(v):
        return v.reshape(SJ, P).T

    dt = np.broadcast_to(sq["log_dt"][0][:, None], (NG, NS))
    a["lam"] = np.stack([states(sq["lam_re"][0]), states(sq["lam_im"][0]), states(dt)], axis=1)
    bt = np.zeros((4, 2, GC, CT, 4, 2, 2, NS), np.float32)
    ct = np.zeros((2, NS, SJ, 2, 2, GC), np.float32)
    for x, (bn, cn) in enumerate((("ssm_b_re", "ssm_c_re"), ("ssm_b_im", "ssm_c_im"))):
        bg = sq[bn][0].reshape(CT, 4, 2, NS, GC)
        cg = sq[cn][0].reshape(SJ, 2, GC, NS)
        for g in range(2):
            for j in range(4):
                bt[j, g, :, :, j, x, g, :] = bg[:, j, g].transpose(2, 0, 1)
            ct[g, :, :, x, g, :] = cg[:, g].transpose(2, 0, 1)
    a["Bt"] = bt.reshape(P, SJ, 2, P)
    a["Ct"] = ct.reshape(P, SJ, 2, 32)
    a["h0"] = np.stack([sq[n][0].reshape(NB, SJ, P).transpose(2, 1, 0) for n in ("state_ssm_re", "state_ssm_im")], axis=1)
    kc = sq["cache_k"][0].reshape(NB, PAST, AW)[:, order]
    vc = sq["cache_v"][0].reshape(NB, PAST, AW)[:, order]
    a["kc"] = kc.transpose(0, 2, 1).reshape(NB, CT, P, PAST).transpose(0, 2, 1, 3)
    a["vc"] = vc.reshape(NB, PAST // P, P, AW).transpose(0, 2, 1, 3)
    a["keysT"] = np.stack([sq["sub_keys1"][0].T, sq["sub_keys2"][0].T], axis=1)
    a["uv"] = np.concatenate([sq["peer_u"][0], sq["peer_v"][0]], axis=1)

    slopes = 2.0 ** (-8.0 * np.arange(1, NH + 1) / NH)
    d = np.arange(P)[:, None] - np.arange(SEQ)[None, :] + (SEQ - P)
    a["pbias"] = np.stack([bias_of(d, s) for s in slopes], axis=1)
    t = np.arange(NT)
    cache_d = PAST + t[:, None] - order[None, :NK]
    own = t[:, None] - t[None, :]
    sb = np.full((NH, NT, NK + NB * ST), -1.0e30, np.float32)
    for h, s in enumerate(slopes):
        sb[h, :, :NK] = bias_of(cache_d, s)
        for b in range(NB):
            sb[h, :, NK + b * ST + b * NT:NK + b * ST + (b + 1) * NT] = bias_of(own, s)
    a["sbias"] = sb.reshape(ST, -1)
    a["ident"] = np.eye(P, dtype=np.float32)
    a["fold"] = np.tile(np.eye(ST, dtype=np.float32), (2, 1))
    a["iota"] = spread(np.arange(PK, dtype=np.float32))
    return {k: np.ascontiguousarray(v) for k, v in a.items()}


def kernel(**inputs):
    import concourse.bacc as bacc
    from concourse.bass_utils import run_bass_kernel_spmd as run

    nc = bacc.Bacc("TRN2", target_bir_lowering=False, num_devices=1)
    arrays = layouts(inputs)
    A = {n: nc.dram_tensor("d_" + n, v.shape, mybir.dt.from_np(v.dtype), kind="ExternalInput").ap() for n, v in arrays.items()}
    made = {"y": (TOK, D), "k_out": (P, CT, TOK), "v_out": (TOK, AW), "stp_out": (P, 2, SJ), "sts_out": (P, 2, SJ, NB)}
    for n, shape in made.items():
        A[n] = nc.dram_tensor("d_" + n, shape, F32, kind="ExternalOutput").ap()
    build(nc, A)
    r = run(nc, [{"d_" + n: v for n, v in arrays.items()}], core_ids=[0]).results[0]
    r = {n: r["d_" + n] for n in made}
    y, v = r["y"], r["v_out"]
    k = r["k_out"].transpose(1, 0, 2).reshape(AW, TOK).T
    stp = r["stp_out"].transpose(1, 2, 0).reshape(2, 1, 1, NG, NS)
    sts = r["sts_out"].transpose(1, 3, 2, 0).reshape(2, 1, NB, NG, NS)
    return (y[:SEQ].reshape(1, SEQ, D), y[SEQ:].reshape(NB, NT, D),
            k[:SEQ].reshape(1, 1, SEQ, NH, HD), v[:SEQ].reshape(1, 1, SEQ, NH, HD),
            stp[0], stp[1],
            k[SEQ:].reshape(1, NB, NT, NH, HD), v[SEQ:].reshape(1, NB, NT, NH, HD),
            sts[0], sts[1])
```
